# Optimizing a Trainium2 kernel written in Bass

```python
import math
import functools
import jax
import jax.numpy as jnp
from jax import lax
import numpy as np

D_MODEL = 1024
BATCH = 1
SEQ = 512
DEPTH = 1
DEC_BATCH = 8
DEC_SEQ = 8
PAST_LEN = 4096
PAGE_SIZE = 128

D_MIX = D_MODEL
D_ATTN = D_MIX // 2
D_SSM = D_MIX - D_ATTN
HEAD_DIM = 64
N_HEADS = D_ATTN // HEAD_DIM
N_KV_HEADS = N_HEADS
ATTN_SCALE = HEAD_DIM ** -0.5
Q_BLOCK = 128
FORGET_BIAS_INIT = 3.0
SSM_GROUP = 16
N_SSM_GROUPS = D_SSM // SSM_GROUP
SSM_STATE = 64
DT_MIN = 1e-3
DT_MAX = 1e-1
N_EXPERTS = 64
TOP_K = 8
D_EXPERT = 256
D_SHARED = 256
ROUTE_SCALE = 2.5
ROUTER_BIAS_SCALE = 0.01
MOE_BLOCK = 128
RMS_EPS = 1e-6
IN_SPLITS = (D_ATTN, 2 * D_ATTN, 3 * D_ATTN, 3 * D_ATTN + N_HEADS)
D_IN = 3 * D_ATTN + N_HEADS + D_SSM

kernel_name = 'hymba_fox_s5_moe_step'

def rms_norm(x, w):
    x32 = x.astype(jnp.float32)
    y = x32 * lax.rsqrt(jnp.mean(x32 * x32, axis=-1, keepdims=True) + RMS_EPS)
    return (y * w.astype(jnp.float32)).astype(x.dtype)

def fox_attend(q, c_q, q_pos, k, v, c_k, k_pos):
    s = jnp.einsum('bqhd,bkhd->bhqk', q.astype(jnp.float32), k.astype(jnp.float32)) * ATTN_SCALE
    bias = jnp.transpose(c_q, (0, 2, 1))[:, :, :, None] - jnp.transpose(c_k, (0, 2, 1))[:, :, None, :]
    causal = k_pos[None, :] <= q_pos[:, None]
    s = jnp.where(causal[None, None], s + bias, -jnp.inf)
    p = jax.nn.softmax(s, axis=-1)
    return jnp.einsum('bhqk,bkhd->bqhd', p, v.astype(jnp.float32)).astype(v.dtype)

def fox_prompt(q, k, v, logf):
    bsz, length = q.shape[0], q.shape[1]
    n_blk = length // Q_BLOCK
    c = jnp.cumsum(logf, axis=1)
    qb = q.reshape(bsz, n_blk, Q_BLOCK, N_HEADS, HEAD_DIM).transpose(1, 0, 2, 3, 4)
    cb = c.reshape(bsz, n_blk, Q_BLOCK, N_HEADS).transpose(1, 0, 2, 3)
    k_pos = jnp.arange(length)

    def block(args):
        q_i, c_i, i = args
        q_pos = i * Q_BLOCK + jnp.arange(Q_BLOCK)
        return fox_attend(q_i, c_i, q_pos, k, v, c, k_pos)

    o = lax.map(block, (qb, cb, jnp.arange(n_blk)))
    return o.transpose(1, 0, 2, 3, 4).reshape(bsz, length, N_HEADS * HEAD_DIM)

def fox_sample(q, k_new, v_new, logf_new, cache_k, cache_v, cache_logf, page_table, layer):
    n_new = q.shape[1]
    past = page_table.shape[1] * PAGE_SIZE
    q_pos = past + jnp.arange(n_new)
    k_pos = jnp.arange(past + n_new)

    def one_seq(args):
        pages, q_b, k_b, v_b, lf_b = args
        k_all = jnp.concatenate([cache_k[layer, pages].reshape(past, N_KV_HEADS, HEAD_DIM),
                                 k_b.astype(cache_k.dtype)], axis=0)
        v_all = jnp.concatenate([cache_v[layer, pages].reshape(past, N_KV_HEADS, HEAD_DIM),
                                 v_b.astype(cache_v.dtype)], axis=0)
        lf_all = jnp.concatenate([cache_logf[layer, pages].reshape(past, N_HEADS).astype(jnp.float32),
                                  lf_b], axis=0)
        c = jnp.cumsum(lf_all, axis=0)
        o = fox_attend(q_b[None], c[None, past:], q_pos, k_all[None], v_all[None], c[None], k_pos)
        return o[0]

    o = lax.map(one_seq, (page_table, q, k_new, v_new, logf_new))
    return o.reshape(q.shape[0], n_new, N_HEADS * HEAD_DIM).astype(q.dtype)

def _linear_combine(e1, e2):
    a1, b1 = e1
    a2, b2 = e2
    return a2 * a1, a2 * b1 + b2

def s5_scan(u, h0_re, h0_im, p):
    bsz, length, _ = u.shape
    f32 = jnp.float32
    u32 = u.astype(f32).reshape(bsz, length, N_SSM_GROUPS, SSM_GROUP)
    lam = lax.complex(p['lambda_re'].astype(f32), p['lambda_im'].astype(f32))
    dt = jnp.exp(p['log_dt'].astype(f32))[:, None]
    lam_bar = jnp.exp(lam * dt)
    b_bar = ((lam_bar - 1.0) / lam)[:, :, None] * lax.complex(p['b_re'].astype(f32), p['b_im'].astype(f32))
    c_mat = lax.complex(p['c_re'].astype(f32), p['c_im'].astype(f32))
    bu = jnp.einsum('gpc,blgc->blgp', b_bar, u32.astype(jnp.complex64))
    h0 = lax.complex(h0_re.astype(f32), h0_im.astype(f32))[:, None]
    elems_b = jnp.concatenate([h0, bu], axis=1)
    elems_a = jnp.broadcast_to(lam_bar, (1, length + 1) + lam_bar.shape)
    _, h = lax.associative_scan(_linear_combine, (elems_a, elems_b), axis=1)
    h = h[:, 1:]
    y = jnp.real(jnp.einsum('gcp,blgp->blgc', c_mat, h)) \
        + p['d_skip'].astype(f32).reshape(N_SSM_GROUPS, SSM_GROUP) * u32
    return y.reshape(bsz, length, D_SSM), h[:, -1]

def ssm_branch(u, h0_re, h0_im, p):
    y, h_last = s5_scan(u, h0_re, h0_im, p)
    z = jax.nn.gelu(y)
    out = z * jax.nn.sigmoid(z @ p['w_glu'].astype(jnp.float32) + p['b_glu'].astype(jnp.float32))
    return out.astype(u.dtype), h_last

def moe_ffn(h, p):
    n_tok = h.shape[0]
    score = jax.nn.sigmoid(jnp.dot(h.astype(jnp.float32), p['w_router'].astype(jnp.float32)))
    _, idx = lax.top_k(score + p['router_bias'].astype(jnp.float32), TOP_K)
    g = jnp.take_along_axis(score, idx, axis=-1)
    g = ROUTE_SCALE * g / jnp.sum(g, axis=-1, keepdims=True)
    n_slots = n_tok * TOP_K
    e_flat = idx.reshape(-1)
    order = jnp.argsort(e_flat)
    e_sorted = e_flat[order]
    tok_sorted = (order // TOP_K).astype(jnp.int32)
    g_sorted = g.reshape(-1)[order]
    counts = jnp.bincount(e_flat, length=N_EXPERTS)
    start = jnp.cumsum(counts) - counts
    padded = (counts + MOE_BLOCK - 1) // MOE_BLOCK * MOE_BLOCK
    pend = jnp.cumsum(padded)
    pstart = pend - padded
    dest = pstart[e_sorted] + jnp.arange(n_slots) - start[e_sorted]
    n_blk = -(-n_slots // MOE_BLOCK) + N_EXPERTS
    tok_buf = jnp.zeros((n_blk * MOE_BLOCK,), jnp.int32).at[dest].set(tok_sorted)
    gate_buf = jnp.zeros((n_blk * MOE_BLOCK,), jnp.float32).at[dest].set(g_sorted)
    blk_expert = jnp.minimum(jnp.searchsorted(pend, jnp.arange(n_blk) * MOE_BLOCK, side='right'),
                             N_EXPERTS - 1)
    w_gate_e, w_up_e, w_down_e = p['w_gate_e'], p['w_up_e'], p['w_down_e']

    def body(acc, blk):
        tb, gb, e = blk
        xb = h[tb]
        a = jax.nn.silu(xb @ w_gate_e[e]) * (xb @ w_up_e[e])
        yb = (a @ w_down_e[e]).astype(jnp.float32)
        return acc.at[tb].add(yb * gb[:, None]), None

    acc, _ = lax.scan(body, jnp.zeros((n_tok, D_MODEL), jnp.float32),
                      (tok_buf.reshape(n_blk, MOE_BLOCK), gate_buf.reshape(n_blk, MOE_BLOCK), blk_expert))
    shared = (jax.nn.silu(h @ p['w_gate_s']) * (h @ p['w_up_s'])) @ p['w_down_s']
    return (acc + shared.astype(jnp.float32)).astype(h.dtype)

def trunk_layer(x, attn_fn, h0_re, h0_im, p):
    bsz, length, _ = x.shape
    hn = rms_norm(x, p['norm_mix_w'])
    q, k, v, f_logit, u = jnp.split(hn @ p['w_in'], IN_SPLITS, axis=-1)
    q = rms_norm(q.reshape(bsz, length, N_HEADS, HEAD_DIM), p['q_norm_w'])
    k = rms_norm(k.reshape(bsz, length, N_KV_HEADS, HEAD_DIM), p['k_norm_w'])
    v = v.reshape(bsz, length, N_KV_HEADS, HEAD_DIM)
    logf = jax.nn.log_sigmoid(f_logit.astype(jnp.float32) + p['b_forget'].astype(jnp.float32))
    attn = attn_fn(q, k, v, logf)
    ssm, h_last = ssm_branch(u, h0_re, h0_im, p)
    mix = jnp.concatenate([rms_norm(attn, p['attn_out_norm_w']), rms_norm(ssm, p['ssm_out_norm_w'])], axis=-1)
    x = x + (mix @ p['w_out']).astype(x.dtype)
    ffn = moe_ffn(rms_norm(x, p['norm_ffn_w']).reshape(bsz * length, D_MODEL), p)
    x = x + ffn.reshape(bsz, length, D_MODEL).astype(x.dtype)
    return x, k, v, logf, jnp.real(h_last), jnp.imag(h_last)

def setup_inputs(seed: int = 0) -> dict:
    key = jax.random.key(seed)
    ks = jax.random.split(key, 36)
    f32 = jnp.float32
    n_pages = PAST_LEN // PAGE_SIZE
    n_used = DEC_BATCH * n_pages
    n_pool = n_used + max(1, n_used // 4)

    def nrm(k, shape, scale=1.0):
        return scale * jax.random.normal(k, shape, f32)

    def gain(k, shape):
        return 1.0 + nrm(k, shape, 0.02)

    page_table = jax.random.permutation(ks[5], n_pool)[:n_used].reshape(DEC_BATCH, n_pages).astype(jnp.int32)
    ssm_n = jnp.arange(SSM_STATE, dtype=f32)
    return {
        'x_prompt': nrm(ks[0], (BATCH, SEQ, D_MODEL)),
        'x_sample': nrm(ks[1], (DEC_BATCH, DEC_SEQ, D_MODEL)),
        'cache_k': nrm(ks[2], (DEPTH, n_pool, PAGE_SIZE, N_KV_HEADS, HEAD_DIM)),
        'cache_v': nrm(ks[3], (DEPTH, n_pool, PAGE_SIZE, N_KV_HEADS, HEAD_DIM)),
        'cache_logf': jax.nn.log_sigmoid(FORGET_BIAS_INIT + nrm(ks[4], (DEPTH, n_pool, PAGE_SIZE, N_HEADS))),
        'page_table': page_table,
        'state_ssm_re': nrm(ks[6], (DEPTH, DEC_BATCH, N_SSM_GROUPS, SSM_STATE), 0.5),
        'state_ssm_im': nrm(ks[7], (DEPTH, DEC_BATCH, N_SSM_GROUPS, SSM_STATE), 0.5),
        'norm_mix_w': gain(ks[8], (DEPTH, D_MODEL)),
        'w_in': nrm(ks[9], (DEPTH, D_MODEL, D_IN), D_MODEL ** -0.5),
        'b_forget': FORGET_BIAS_INIT + nrm(ks[10], (DEPTH, N_HEADS), 0.5),
        'q_norm_w': gain(ks[11], (DEPTH, HEAD_DIM)),
        'k_norm_w': gain(ks[12], (DEPTH, HEAD_DIM)),
        'lambda_re': -0.5 + nrm(ks[13], (DEPTH, N_SSM_GROUPS, SSM_STATE), 0.01),
        'lambda_im': math.pi * ssm_n + nrm(ks[14], (DEPTH, N_SSM_GROUPS, SSM_STATE), 0.01),
        'log_dt': jax.random.uniform(ks[15], (DEPTH, N_SSM_GROUPS), f32, math.log(DT_MIN), math.log(DT_MAX)),
        'b_re': nrm(ks[16], (DEPTH, N_SSM_GROUPS, SSM_STATE, SSM_GROUP), (2 * SSM_GROUP) ** -0.5),
        'b_im': nrm(ks[17], (DEPTH, N_SSM_GROUPS, SSM_STATE, SSM_GROUP), (2 * SSM_GROUP) ** -0.5),
        'c_re': nrm(ks[18], (DEPTH, N_SSM_GROUPS, SSM_GROUP, SSM_STATE), SSM_STATE ** -0.5),
        'c_im': nrm(ks[19], (DEPTH, N_SSM_GROUPS, SSM_GROUP, SSM_STATE), SSM_STATE ** -0.5),
        'd_skip': nrm(ks[20], (DEPTH, D_SSM)),
        'w_glu': nrm(ks[21], (DEPTH, D_SSM, D_SSM), D_SSM ** -0.5),
        'b_glu': nrm(ks[22], (DEPTH, D_SSM), 0.01),
        'attn_out_norm_w': gain(ks[23], (DEPTH, D_ATTN)),
        'ssm_out_norm_w': gain(ks[24], (DEPTH, D_SSM)),
        'w_out': nrm(ks[25], (DEPTH, D_MIX, D_MODEL), D_MIX ** -0.5),
        'norm_ffn_w': gain(ks[26], (DEPTH, D_MODEL)),
        'w_router': nrm(ks[27], (DEPTH, D_MODEL, N_EXPERTS), D_MODEL ** -0.5),
        'router_bias': nrm(ks[28], (DEPTH, N_EXPERTS), ROUTER_BIAS_SCALE),
        'w_gate_e': nrm(ks[29], (DEPTH, N_EXPERTS, D_MODEL, D_EXPERT), D_MODEL ** -0.5),
        'w_up_e': nrm(ks[30], (DEPTH, N_EXPERTS, D_MODEL, D_EXPERT), D_MODEL ** -0.5),
        'w_down_e': nrm(ks[31], (DEPTH, N_EXPERTS, D_EXPERT, D_MODEL), D_EXPERT ** -0.5),
        'w_gate_s': nrm(ks[32], (DEPTH, D_MODEL, D_SHARED), D_MODEL ** -0.5),
        'w_up_s': nrm(ks[33], (DEPTH, D_MODEL, D_SHARED), D_MODEL ** -0.5),
        'w_down_s': nrm(ks[34], (DEPTH, D_SHARED, D_MODEL), D_SHARED ** -0.5),
    }

def reference(x_prompt, x_sample, cache_k, cache_v, cache_logf, page_table, state_ssm_re, state_ssm_im,
              norm_mix_w, w_in, b_forget, q_norm_w, k_norm_w, lambda_re, lambda_im, log_dt,
              b_re, b_im, c_re, c_im, d_skip, w_glu, b_glu, attn_out_norm_w, ssm_out_norm_w, w_out,
              norm_ffn_w, w_router, router_bias, w_gate_e, w_up_e, w_down_e, w_gate_s, w_up_s, w_down_s):
    x_p, x_s = x_prompt, x_sample
    k_p, v_p, lf_p, re_p, im_p = [], [], [], [], []
    k_s, v_s, lf_s, re_s, im_s = [], [], [], [], []
    for l in range(DEPTH):
        p = {
            'norm_mix_w': norm_mix_w[l], 'w_in': w_in[l], 'b_forget': b_forget[l],
            'q_norm_w': q_norm_w[l], 'k_norm_w': k_norm_w[l],
            'lambda_re': lambda_re[l], 'lambda_im': lambda_im[l], 'log_dt': log_dt[l],
            'b_re': b_re[l], 'b_im': b_im[l], 'c_re': c_re[l], 'c_im': c_im[l], 'd_skip': d_skip[l],
            'w_glu': w_glu[l], 'b_glu': b_glu[l],
            'attn_out_norm_w': attn_out_norm_w[l], 'ssm_out_norm_w': ssm_out_norm_w[l], 'w_out': w_out[l],
            'norm_ffn_w': norm_ffn_w[l], 'w_router': w_router[l], 'router_bias': router_bias[l],
            'w_gate_e': w_gate_e[l], 'w_up_e': w_up_e[l], 'w_down_e': w_down_e[l],
            'w_gate_s': w_gate_s[l], 'w_up_s': w_up_s[l], 'w_down_s': w_down_s[l],
        }
        h0 = jnp.zeros((x_p.shape[0], N_SSM_GROUPS, SSM_STATE), jnp.float32)
        x_p, kk, vv, lf, hr, hi = trunk_layer(x_p, fox_prompt, h0, h0, p)
        k_p.append(kk); v_p.append(vv); lf_p.append(lf); re_p.append(hr); im_p.append(hi)
        attn_sample = functools.partial(fox_sample, cache_k=cache_k, cache_v=cache_v, cache_logf=cache_logf,
                                        page_table=page_table, layer=l)
        x_s, kk, vv, lf, hr, hi = trunk_layer(x_s, attn_sample, state_ssm_re[l], state_ssm_im[l], p)
        k_s.append(kk); v_s.append(vv); lf_s.append(lf); re_s.append(hr); im_s.append(hi)
    return (x_p, x_s, jnp.stack(k_p), jnp.stack(v_p), jnp.stack(lf_p), jnp.stack(re_p), jnp.stack(im_p),
            jnp.stack(k_s), jnp.stack(v_s), jnp.stack(lf_s), jnp.stack(re_s), jnp.stack(im_s))


_drawn_inputs = setup_inputs


def setup_inputs(seed=0):
    import zlib

    import numpy as np

    out = dict(_drawn_inputs(seed))
    spreads = {}
    factors = {'lambda_re': 3.952, 'b_glu': 2.72}
    for name, (base, spread) in spreads.items():
        noise = np.random.default_rng([zlib.crc32(name.encode()), seed]).standard_normal(out[name].shape)
        drawn = base * np.exp(spread * noise) if base else spread * noise
        out[name] = jnp.asarray(drawn.astype(out[name].dtype))
    for name, factor in factors.items():
        out[name] = (out[name] * factor).astype(out[name].dtype)
    return out
```

```python
import concourse.bass as bass
from concourse import mybir
from contextlib import ExitStack
import numpy as np

F32 = mybir.dt.float32
I32 = mybir.dt.int32
ALU = mybir.AluOpType
ACT = mybir.ActivationFunctionType
AX = mybir.AxisListType

P = 128
D = 1024
SEQ = 512
DEC_B, DEC_S = 8, 8
T_S = DEC_B * DEC_S
T = SEQ + T_S
PT = SEQ // P
TT = PT + 1
KD = D // P
DA = 512
HD = 64
NH = 8
HP = NH // 2
KA = DA // P
DS = 512
KS = DS // P
GC = 16
NG = DS // GC
NS = 64
PAGE = 128
NPG = 32
N_POOL = 320
NE = 64
TOPK = 8
DE = 256
D_IN = 3 * DA + NH + DS
EPS = 1e-6
MASKED = -1e30
L = 8
NC_P = SEQ // L
NCH = T // L


class Memory:
    pass


def rows(t):
    return P if t < PT else T_S


def cols(t):
    return slice(t * P, t * P + rows(t))


def end_stage(nc, m):
    nc.clear_and_free_semaphores(m.sems)
    m.sems.clear()
    nc.all_engine_barrier()


def constants(nc, m):
    sb = nc.alloc_sbuf_tensor
    m.ident = sb("ident", [P, P], F32)
    m.ones = sb("ones", [P, P], F32)
    m.tri_incl = sb("tri_incl", [P, P], F32)
    m.tri_strict = sb("tri_strict", [P, P], F32)
    m.causal = sb("causal", [P, P], F32)
    m.tri_seq = sb("tri_seq", [T_S, T_S], F32)

    with nc.Block(no_gpsimd_drain=True) as block:

        @block.gpsimd
        def _(pool):
            for tile, value in ((m.ident, 0.0), (m.ones, 1.0), (m.tri_incl, 1.0), (m.tri_strict, 1.0),
                                (m.causal, 0.0), (m.tri_seq, 1.0)):
                pool.memset(tile[:, :], value)
            pool.drain()

            def select(view, op, fill, base, pattern, cm):
                pool.affine_select(out=view, in_=view, compare_op=op, fill=fill, base=base,
                                   pattern=pattern, channel_multiplier=cm)

            select(m.ident[:, :], ALU.not_equal, 1.0, 0, [[-1, P]], 1)
            select(m.tri_incl[:, :], ALU.is_ge, 0.0, 0, [[1, P]], -1)
            select(m.tri_strict[:, :], ALU.is_gt, 0.0, 0, [[1, P]], -1)
            select(m.causal[:, :], ALU.is_ge, MASKED, 0, [[-1, P]], 1)
            select(m.tri_seq[:, :], ALU.is_ge, 0.0, 0, [[1, T_S]], -1)
            pool.drain()
            select(m.tri_seq[:, :].rearrange("k (b i) -> k b i", i=DEC_S), ALU.is_ge, 0.0, 0, [[-DEC_S, DEC_B], [0, DEC_S]], 1)
            pool.drain()


def project(nc, a, o, m):
    sb, sem = nc.alloc_sbuf_tensor, m.sem
    m.xres = sb("xres", [P, TT, D], F32)
    m.columns = sb("columns", [P, 32], F32)
    m.kT = sb("kT", [P, HP, T], F32)
    m.qT = sb("qT", [P, HP, T], F32)
    m.v = sb("v", [P, TT, DA], F32)
    m.uT = sb("uT", [P, KS, T], F32)
    m.mixT = sb("mixT", [P, KA + KS, T], F32)
    m.logf = sb("logf", [P, TT, NH], F32)
    m.rows_bc = sb("rows_bc", [P, 4 * 64], F32)
    NORM_MIX, NORM_FFN, ATTN_OUT, SSM_OUT, B_GLU, D_SKIP = 0, 8, 16, 20, 24, 28
    m.col = dict(norm_mix=NORM_MIX, norm_ffn=NORM_FFN, mix_out=ATTN_OUT, b_glu=B_GLU, d_skip=D_SKIP)
    m.qw = m.rows_bc[:, 0:64]
    m.kw = m.rows_bc[:, 64:128]
    m.router_bias = m.rows_bc[:, 128:192]
    m.b_forget = m.rows_bc[:, 192:200]
    m.log_dt = m.rows_bc[:, 200:232]

    with (
        nc.sbuf_tensor("vec_rows", [32, P], F32) as vec_rows,
        nc.sbuf_tensor("w_in", [P, KD, D_IN], F32) as w_in,
        nc.sbuf_tensor("xn", [P, 2, D], F32) as xn,
        nc.sbuf_tensor("xT", [P, KD, T], F32) as xT,
        nc.sbuf_tensor("qkn", [P, 2, 2, DA], F32) as qkn,
        nc.sbuf_tensor("sq", [P, 2, 2 * DA], F32) as sq,
        nc.sbuf_tensor("stat", [P, 3, TT], F32) as stat,
        nc.sbuf_tensor("hstat", [P, 2, 3, 16], F32) as hstat,
        nc.sbuf_tensor("fl", [P, 3, TT * NH], F32) as fl,
        nc.psum_tensor("tr", [P, 2, 512], F32) as tr,
        nc.psum_tensor("pq", [P, 2, 512], F32) as pq,
        nc.psum_tensor("pv", [P, 512], F32) as pv,
        nc.psum_tensor("pf", [P, 512], F32) as pf,
        nc.psum_tensor("pu", [P, 2, 512], F32) as pu,
    ):
        x_loaded = [sem(f"x_loaded{t}") for t in range(TT)]
        vec_loaded, w_loaded = sem("vec_loaded"), sem("w_in_loaded")
        sumsq_done, ms_done, root_done, xn_done = sem("sumsq"), sem("ms"), sem("root"), sem("xn_done")
        col_tr, col_done = sem("col_tr"), sem("col_done")
        xn_tr, xT_done = sem("xn_tr"), sem("xT_done")
        q_mm, v_mm, f_mm, u_mm = sem("q_mm"), sem("v_mm"), sem("f_mm"), sem("u_mm")
        sq_done, v_done, f_done, u_done = sem("sq_done"), sem("v_done"), sem("f_done"), sem("u_done")
        hms_done, hroot_done, qkn_done = sem("hms"), sem("hroot"), sem("qkn_done")
        q_taken, qk_tr, qkT_done = sem("q_taken"), sem("qk_tr"), sem("qkT_done")
        fabs_done, fln_done, logf_done, stored = sem("fabs"), sem("fln"), sem("logf_done"), sem("stored_a")
        k_stored = [sem(f"k_stored{b}") for b in range(2)]

        with nc.Block(no_gpsimd_drain=True) as block:

            @block.sync
            def _(sp):
                for t in range(TT):
                    src = a["x_prompt"][0, t * P:(t + 1) * P, :] if t < PT else a["x_sample"].rearrange("b s d -> (b s) d")
                    sp.dma_start(m.xres[0:rows(t), t, :], src).then_inc(x_loaded[t], 16)
                for k in range(KD):
                    sp.dma_start(w_in[:, k, :], a["w_in"][0, k * P:(k + 1) * P, :]).then_inc(w_loaded, 16)
                for t in range(TT):
                    n = rows(t)
                    sp.wait_ge(qkn_done, t + 1)
                    dst = o["k_prompt"][0, 0, t * P:(t + 1) * P].rearrange("s h d -> s (h d)") if t < PT \
                        else o["k_sample"][0].rearrange("b s h d -> (b s) (h d)")
                    sp.dma_start(dst, qkn[0:n, t % 2, 1, :]).then_inc(k_stored[t % 2], 16)
                    sp.wait_ge(v_done, t + 1)
                    dst = o["v_prompt"][0, 0, t * P:(t + 1) * P].rearrange("s h d -> s (h d)") if t < PT \
                        else o["v_sample"][0].rearrange("b s h d -> (b s) (h d)")
                    sp.dma_start(dst, m.v[0:n, t, :]).then_inc(stored, 16)
                sp.wait_ge(logf_done, 1)
                sp.dma_start(o["logf_prompt"][0, 0].rearrange("(t p) h -> p t h", p=P), m.logf[:, 0:PT, :]).then_inc(stored, 16)
                sp.dma_start(o["logf_sample"][0].rearrange("b s h -> (b s) h"), m.logf[0:T_S, PT, :]).then_inc(stored, 16)
                sp.wait_ge(k_stored[0], 16 * ((TT + 1) // 2))
                sp.wait_ge(k_stored[1], 16 * (TT // 2))
                sp.wait_ge(stored, 16 * (TT + 2))

            @block.scalar
            def _(act):
                for name, at, n in (("norm_mix_w", NORM_MIX, 8), ("norm_ffn_w", NORM_FFN, 8), ("attn_out_norm_w", ATTN_OUT, 4),
                                    ("ssm_out_norm_w", SSM_OUT, 4), ("b_glu", B_GLU, 4), ("d_skip", D_SKIP, 4)):
                    act.dma_start(vec_rows[at:at + n, :], a[name][0].rearrange("(k p) -> k p", p=P)).then_inc(vec_loaded, 16)
                for name, dst in (("q_norm_w", m.qw), ("k_norm_w", m.kw), ("router_bias", m.router_bias),
                                  ("b_forget", m.b_forget), ("log_dt", m.log_dt)):
                    act.dma_start(dst, a[name][0].partition_broadcast(P)).then_inc(vec_loaded, 16)
                for t in range(TT):
                    n = rows(t)
                    act.wait_ge(x_loaded[t], 16)
                    if t:
                        act.drain()
                    act.activation(sq[0:n, 0, :], m.xres[0:n, t, :], ACT.Square,
                                   accum_out=stat[0:n, 0, t:t + 1]).then_inc(sumsq_done, 1)
                act.wait_ge(ms_done, 1)
                act.activation(stat[:, 2, 0:PT], stat[:, 1, 0:PT], ACT.Sqrt)
                act.activation(stat[0:T_S, 2, PT:TT], stat[0:T_S, 1, PT:TT], ACT.Sqrt).then_inc(root_done, 1)
                act.wait_ge(col_tr, 1)
                act.copy(m.columns[:, :], pv[:, 0:32]).then_inc(col_done, 1)

                def transposed(t):
                    n = rows(t)
                    act.wait_ge(qk_tr, t + 1)
                    act.activation(m.qT[:, :, cols(t)], tr[:, 0, :].rearrange("p (h n) -> p h n", n=P)[:, :, 0:n], ACT.Copy, scale=HD ** -0.5)
                    act.activation(m.kT[:, :, cols(t)], tr[:, 1, :].rearrange("p (h n) -> p h n", n=P)[:, :, 0:n], ACT.Copy).then_inc(qkT_done, 1)

                for t in range(TT):
                    n, b = rows(t), t % 2
                    act.wait_ge(q_mm, t + 1)
                    if t >= 1:
                        act.wait_ge(hms_done, t)
                    act.activation(sq[0:n, 1, :].rearrange("p (a n) -> p a n", a=2), pq[0:n, :, :], ACT.Square).then_inc(sq_done, 1)
                    act.wait_ge(v_mm, t + 1)
                    act.copy(m.v[0:n, t, :], pv[0:n, :]).then_inc(v_done, 1)
                    act.wait_ge(hms_done, t + 1)
                    act.activation(hstat[0:n, b, 2, :], hstat[0:n, b, 1, :], ACT.Sqrt).then_inc(hroot_done, 1)
                    if t >= 1:
                        transposed(t - 1)
                transposed(TT - 1)
                act.wait_ge(fabs_done, 1)
                for r, c in ((P, slice(0, PT * NH)), (T_S, slice(PT * NH, TT * NH))):
                    act.activation(fl[0:r, 1, c], fl[0:r, 1, c], ACT.Exp, scale=-1.0)
                act.drain()
                act.activation(fl[:, 2, 0:PT * NH], fl[:, 1, 0:PT * NH], ACT.Ln, bias=1.0)
                act.activation(fl[0:T_S, 2, PT * NH:], fl[0:T_S, 1, PT * NH:], ACT.Ln, bias=1.0).then_inc(fln_done, 1)
                for i in range(2 * KS):
                    c, part = i // 2, i % 2
                    act.wait_ge(u_mm, i + 1)
                    if part == 0:
                        act.copy(m.uT[:, c, 0:SEQ], pu[:, 0, :]).then_inc(u_done, 1)
                    else:
                        act.copy(m.uT[:, c, SEQ:T], pu[:, 1, 0:T_S]).then_inc(u_done, 1)

            @block.vector
            def _(dve):
                dve.wait_ge(sumsq_done, TT)
                dve.tensor_scalar(stat[:, 1, 0:PT], stat[:, 0, 0:PT], 1.0 / D, EPS, ALU.mult, ALU.add)
                dve.tensor_scalar(stat[0:T_S, 1, PT:TT], stat[0:T_S, 0, PT:TT], 1.0 / D, EPS, ALU.mult, ALU.add).then_inc(ms_done, 1)
                dve.wait_ge(root_done, 1)
                dve.reciprocal(stat[:, 0, 0:PT], stat[:, 2, 0:PT])
                dve.reciprocal(stat[0:T_S, 0, PT:TT], stat[0:T_S, 2, PT:TT])
                dve.drain()
                for t in range(TT):
                    n = rows(t)
                    if t >= 2:
                        dve.wait_ge(xn_tr, 2 * (t - 1))
                    dve.tensor_scalar(xn[0:n, t % 2, :], m.xres[0:n, t, :], stat[0:n, 0, t:t + 1], None, ALU.mult).then_inc(xn_done, 1)
                    if t == 0:
                        dve.wait_ge(col_done, 1)
                    for half in range(2):
                        dve.wait_ge(xn_tr, 2 * t + half + 1)
                        w = m.columns[:, NORM_MIX + 4 * half:NORM_MIX + 4 * half + 4].unsqueeze(2).to_broadcast((P, 4, n))
                        dve.tensor_tensor(xT[:, 4 * half:4 * half + 4, cols(t)],
                                          tr[:, half, :].rearrange("p (k n) -> p k n", n=P)[:, :, 0:n], w, ALU.mult).then_inc(xT_done, 1)
                for t in range(TT):
                    n, b = rows(t), t % 2
                    ss, ms, root = (hstat[0:n, b, i, :] for i in range(3))
                    dve.wait_ge(sq_done, t + 1)
                    dve.tensor_reduce(ss, sq[0:n, 1, :].rearrange("p (h d) -> p h d", d=HD), AX.X, ALU.add)
                    dve.drain()
                    dve.tensor_scalar(ms, ss, 1.0 / HD, EPS, ALU.mult, ALU.add).then_inc(hms_done, 1)
                    dve.wait_ge(hroot_done, t + 1)
                    dve.reciprocal(ss, root)
                    if t >= 2:
                        dve.wait_ge(qk_tr, t - 1)
                        dve.wait_ge(k_stored[b], 16 * (t // 2))
                    dve.drain()
                    inv = hstat[0:n, b, 0, :].rearrange("p (a h) -> p a h", a=2).unsqueeze(3).to_broadcast((n, 2, NH, HD))
                    heads = qkn[0:n, b, :, :].rearrange("p a (h d) -> p a h d", d=HD)
                    for i in range(2):
                        last = dve.tensor_tensor(heads[:, i], pq[0:n, i, :].rearrange("p (h d) -> p h d", d=HD), inv[:, i], ALU.mult)
                    last.then_inc(q_taken, 1)
                    dve.drain()
                    for i, w in ((0, m.qw), (1, m.kw)):
                        last = dve.tensor_tensor(heads[:, i], heads[:, i], w[0:n, :].unsqueeze(1).to_broadcast((n, NH, HD)), ALU.mult)
                    last.then_inc(qkn_done, 1)
                    dve.wait_ge(f_mm, t + 1)
                    dve.tensor_tensor(fl[0:n, 0, t * NH:(t + 1) * NH], pf[0:n, 0:NH], m.b_forget[0:n, :], ALU.add).then_inc(f_done, 1)
                dve.drain()
                for r, c in ((P, slice(0, PT * NH)), (T_S, slice(PT * NH, TT * NH))):
                    last = dve.scalar_tensor_tensor(fl[0:r, 1, c], fl[0:r, 0, c], -1.0, fl[0:r, 0, c], ALU.mult, ALU.max)
                last.then_inc(fabs_done, 1)
                dve.wait_ge(fln_done, 1)
                lf = m.logf[:, :, :].rearrange("p t h -> p (t h)")
                for r, c in ((P, slice(0, PT * NH)), (T_S, slice(PT * NH, TT * NH))):
                    last = dve.scalar_tensor_tensor(lf[0:r, c], fl[0:r, 0, c], 0.0, fl[0:r, 2, c], ALU.min, ALU.subtract)
                last.then_inc(logf_done, 1)

            @block.tensor
            def _(pe):
                pe.wait_ge(vec_loaded, 16 * 11)
                pe.transpose(pv[:, 0:32], vec_rows[:, :], m.ident[0:32, 0:32]).then_inc(col_tr, 1)
                for t in range(TT):
                    n = rows(t)
                    pe.wait_ge(xn_done, t + 1)
                    for half in range(2):
                        if t >= 1:
                            pe.wait_ge(xT_done, 2 * (t - 1) + half + 1)
                        for j in range(4):
                            k = 4 * half + j
                            last = pe.transpose(tr[:, half, j * P:j * P + n], xn[0:n, t % 2, k * P:(k + 1) * P], m.ident[0:n, 0:n])
                        last.then_inc(xn_tr, 1)
                pe.wait_ge(xT_done, 2 * TT)
                pe.wait_ge(w_loaded, 16 * KD)
                pe.wait_ge(col_done, 1)

                def over_width(out, n, lhs_of, rhs_of):
                    for k in range(KD):
                        last = pe.matmul(out, lhs_of(k), rhs_of(k), start=(k == 0), stop=(k == KD - 1))
                    return last

                def transposes(t):
                    n = rows(t)
                    pe.wait_ge(qkn_done, t + 1)
                    if t >= 1:
                        pe.wait_ge(qkT_done, t)
                    for i in range(2):
                        for j in range(HP):
                            last = pe.transpose(tr[:, i, j * P:j * P + n], qkn[0:n, t % 2, i, j * P:(j + 1) * P], m.ident[0:n, 0:n])
                    last.then_inc(qk_tr, 1)

                for t in range(TT):
                    n = rows(t)
                    tok = lambda k: xT[:, k, cols(t)]
                    if t >= 1:
                        pe.wait_ge(q_taken, t)
                    for i in range(2):
                        last = over_width(pq[0:n, i, :], n, tok, lambda k: w_in[:, k, i * DA:(i + 1) * DA])
                    last.then_inc(q_mm, 1)
                    if t >= 1:
                        pe.wait_ge(v_done, t)
                    over_width(pv[0:n, :], n, tok, lambda k: w_in[:, k, 2 * DA:3 * DA]).then_inc(v_mm, 1)
                    if t >= 1:
                        pe.wait_ge(f_done, t)
                    over_width(pf[0:n, 0:NH], n, tok, lambda k: w_in[:, k, 3 * DA:3 * DA + NH]).then_inc(f_mm, 1)
                    if t >= 1:
                        transposes(t - 1)
                for c in range(KS):
                    w = lambda k: w_in[:, k, 3 * DA + NH + c * P:3 * DA + NH + (c + 1) * P]
                    if c >= 1:
                        pe.wait_ge(u_done, 2 * c - 1)
                    over_width(pu[:, 0, :], P, w, lambda k: xT[:, k, 0:SEQ]).then_inc(u_mm, 1)
                    if c >= 1:
                        pe.wait_ge(u_done, 2 * c)
                    over_width(pu[:, 1, 0:T_S], P, w, lambda k: xT[:, k, SEQ:T]).then_inc(u_mm, 1)
                    if c == 0:
                        transposes(TT - 1)


def prompt_attention(nc, a, o, m, recurrence):
    sem = m.sem
    UNITS = 2 * PT
    SHARE = (NC_P - 1) // HP
    with (
        nc.sbuf_tensor("c_tok", [P, PT, NH], F32) as c_tok,
        nc.sbuf_tensor("neg_c", [NH, SEQ], F32) as neg_c,
        nc.sbuf_tensor("neg_c_of", [NH, NH, SEQ], F32) as neg_c_of,
        nc.sbuf_tensor("q_pair", [P, SEQ], F32) as q_pair,
        nc.sbuf_tensor("k_pair", [P, SEQ], F32) as k_pair,
        nc.sbuf_tensor("probs", [P, 2, SEQ], F32) as probs,
        nc.sbuf_tensor("probsT", [P, 2, SEQ], F32) as probsT,
        nc.sbuf_tensor("o_pair", [P, PT, P], F32) as o_pair,
        nc.sbuf_tensor("row_stat", [P, 2, 4], F32) as row_stat,
        nc.psum_tensor("ps_s", [P, 2, 512], F32) as ps_s,
        nc.psum_tensor("ps_t", [P, 2, 512], F32) as ps_t,
        nc.psum_tensor("ps_o", [P, 2, 512], F32) as ps_o,
        nc.psum_tensor("ps_c", [P, 512], F32) as ps_c,
    ):
        c_mm, c_sb, cT_mm, c_ready, c_of_ready = sem("c_mm"), sem("c_sb"), sem("cT_mm"), sem("c_ready"), sem("c_of_ready")
        pair_staged = sem("pair_staged")
        s_mm, max_done, probs_done, t_mm, probsT_done = sem("s_mm"), sem("max_done"), sem("probs_done"), sem("t_mm"), sem("probsT_done")
        inv_done, o_mm, o_done, oT_mm, oT_done = sem("inv_done"), sem("o_mm"), sem("o_done"), sem("oT_mm"), sem("oT_done")

        with nc.Block(no_gpsimd_drain=True) as block:

            @block.tensor
            def _(pe):
                pe.sem_inc(s_mm, 1)
                for t in range(PT):
                    for s in range(t + 1):
                        last = pe.matmul(ps_c[:, t * NH:(t + 1) * NH], (m.tri_incl if s == t else m.ones)[:, :],
                                         m.logf[:, s, :], start=(s == 0), stop=(s == t))
                last.then_inc(c_mm, 1)
                pe.wait_ge(c_sb, 1)
                for t in range(PT):
                    last = pe.transpose(ps_o[0:NH, 0, t * P:(t + 1) * P], c_tok[:, t, :], m.ident[:, :])
                last.then_inc(cT_mm, 1)
                pe.wait_ge(c_of_ready, 1)

                def scores(i, u):
                    h, t = divmod(u, PT)
                    n = (t + 1) * P
                    pe.wait_ge(probs_done, i * UNITS + u + 1)
                    pe.matmul(ps_s[:, u % 2, 0:n], q_pair[HD * h:HD * h + HD, t * P:(t + 1) * P], k_pair[HD * h:HD * h + HD, 0:n],
                              start=True, stop=False)
                    pe.matmul(ps_s[:, u % 2, 0:n], m.ones[0:NH, :], neg_c_of[:, 2 * i + h, 0:n], start=False, stop=True).then_inc(s_mm, 1)

                with pe.Fori(0, HP) as i:
                    pe.wait_ge(pair_staged, i + 1)
                    scores(i, 0)
                    for u in range(UNITS):
                        h, t = divmod(u, PT)
                        if u + 1 < UNITS:
                            scores(i, u + 1)
                        pe.wait_ge(probs_done, i * UNITS + u + 3)
                        pe.wait_ge(probsT_done, i * UNITS + u + 1)
                        for k in range(t + 1):
                            last = pe.transpose(ps_t[:, u % 2, k * P:(k + 1) * P], probs[:, u % 2, k * P:(k + 1) * P], m.ident[:, :])
                        last.then_inc(t_mm, 1)
                        pe.wait_ge(probsT_done, i * UNITS + u + 3)
                        pe.wait_ge(o_done, i * UNITS + u + 1)
                        for k in range(t + 1):
                            last = pe.matmul(ps_o[:, u % 2, 0:HD], probsT[:, u % 2, k * P:(k + 1) * P],
                                             m.v[:, k, bass.ds(i * P + h * HD, HD)], start=(k == 0), stop=(k == t))
                        last.then_inc(o_mm, 1)
                    pe.wait_ge(o_done, i * UNITS + UNITS + 2)
                    pe.wait_ge(oT_done, i + 1)
                    for t in range(PT):
                        last = pe.transpose(ps_c[:, t * P:(t + 1) * P], o_pair[:, t, :], m.ident[:, :])
                    last.then_inc(oT_mm, 1)

            @block.gpsimd
            def _(pool):
                recurrence(pool, "start")
                with pool.Fori(0, HP) as i:
                    pool.wait_ge(s_mm, i * UNITS + 1)
                    pool.tensor_copy(q_pair[:, :], m.qT[:, bass.ds(i, 1), 0:SEQ].rearrange("p a n -> p (a n)"))
                    pool.tensor_copy(k_pair[:, :], m.kT[:, bass.ds(i, 1), 0:SEQ].rearrange("p a n -> p (a n)"))
                    pool.drain()
                    pool.sem_inc(pair_staged, 1)
                    recurrence(pool, (i * SHARE, SHARE))
                recurrence(pool, (HP * SHARE, NC_P - 1 - HP * SHARE))
                recurrence(pool, "end")

            @block.scalar
            def _(act):
                act.sem_inc(probs_done, 2)
                act.sem_inc(o_done, 2)
                act.wait_ge(cT_mm, 1)
                act.activation(neg_c[:, :], ps_o[0:NH, 0, :], ACT.Copy, scale=-1.0).then_inc(c_ready, 1)
                with act.Fori(0, HP) as i:
                    def output(u):
                        h, t = divmod(u, PT)
                        act.wait_ge(inv_done, i * UNITS + u + 1)
                        act.wait_ge(o_mm, i * UNITS + u + 1)
                        if u == 0:
                            act.wait_ge(oT_done, i + 1)
                        act.activation(o_pair[:, t, h * HD:(h + 1) * HD], ps_o[:, u % 2, 0:HD], ACT.Copy,
                                       scale=row_stat[:, u % 2, 3:4]).then_inc(o_done, 1)

                    for u in range(UNITS):
                        n = (u % PT + 1) * P
                        act.wait_ge(max_done, i * UNITS + u + 1)
                        act.wait_ge(t_mm, i * UNITS + u + 1)
                        act.activation(probs[:, u % 2, 0:n], ps_s[:, u % 2, 0:n], ACT.Exp, bias=row_stat[:, u % 2, 1:2],
                                       accum_out=row_stat[:, u % 2, 2:3]).then_inc(probs_done, 1)
                        if u:
                            output(u - 1)
                    output(UNITS - 1)

            @block.vector
            def _(dve):
                dve.sem_inc(probsT_done, 2)
                dve.sem_inc(oT_done, 1)
                dve.sem_inc(t_mm, 2)
                dve.wait_ge(c_mm, 1)
                dve.tensor_copy(c_tok[:, :, :], ps_c[:, 0:PT * NH].rearrange("p (t h) -> p t h", h=NH)).then_inc(c_sb, 1)
                dve.wait_ge(c_ready, 1)
                for h in range(NH):
                    last = dve.tensor_scalar(neg_c_of[:, h, :], neg_c[:, :], m.ident[0:NH, h:h + 1], None, ALU.mult)
                last.then_inc(c_of_ready, 1)
                with dve.Fori(0, HP) as i:
                    def transposed(u):
                        n = (u % PT + 1) * P
                        dve.wait_ge(t_mm, i * UNITS + u + 3)
                        dve.tensor_copy(probsT[:, u % 2, 0:n], ps_t[:, u % 2, 0:n]).then_inc(probsT_done, 1)

                    for u in range(UNITS):
                        t = u % PT
                        n = (t + 1) * P
                        stat = row_stat[:, u % 2, :]
                        dve.wait_ge(s_mm, i * UNITS + u + 2)
                        dve.tensor_tensor(ps_s[:, u % 2, t * P:n], ps_s[:, u % 2, t * P:n], m.causal[:, :], ALU.add)
                        dve.drain()
                        dve.tensor_reduce(stat[:, 0:1], ps_s[:, u % 2, 0:n], AX.X, ALU.max)
                        dve.drain()
                        dve.wait_ge(o_done, i * UNITS + u + 1)
                        dve.tensor_scalar(stat[:, 1:2], stat[:, 0:1], -1.0, None, ALU.mult).then_inc(max_done, 1)
                        if u:
                            transposed(u - 1)
                        dve.wait_ge(probs_done, i * UNITS + u + 3)
                        dve.reciprocal(stat[:, 3:4], stat[:, 2:3]).then_inc(inv_done, 1)
                    transposed(UNITS - 1)
                    dve.wait_ge(oT_mm, i + 1)
                    dve.tensor_copy(m.mixT[:, bass.ds(i, 1), 0:SEQ].rearrange("p a n -> p (a n)"), ps_c[:, :]).then_inc(oT_done, 1)


GB = 4
N_GB = NG // GB


def state_space_and_prompt_attention(nc, a, o, m):
    sem = m.sem
    TWO_PI_A = 6.28125
    TWO_PI_B = float(np.float32(2 * np.pi - TWO_PI_A))
    TWO_PI_C = float(2 * np.pi - TWO_PI_A - TWO_PI_B)
    PI_IN = 3.1415925

    u_scr = nc.dram_tensor("u_scr", (DS, L * NCH), F32, kind="Internal").ap()
    y_scr = nc.dram_tensor("y_scr", (DS, L * NCH), F32, kind="Internal").ap()

    with ExitStack() as scope:
        sb = lambda *args: scope.enter_context(nc.sbuf_tensor(*args))
        c_12 = sb("c_12", [P, 2, NG, GC], F32)
        sgn = sb("sgn", [P, 2], F32)
        pow_up = sb("pow_up", [P, 2, NG, 9], F32)
        step_ab = sb("step_ab", [P, 2, 2, NG], F32)
        u_perm = sb("u_perm", [P, KS, L, NCH], F32)
        u_chunk = sb("u_chunk", [P, NG, NCH], F32)
        x_pow = sb("x_pow", [P, 2, GB, P], F32)
        e_end = sb("e_end", [P, NCH, 2, NG], F32)
        h_start = sb("h_start", [P, NCH, 2, NG], F32)
        h_last = sb("h_last", [P, 2, NG], F32)
        h_last_s = sb("h_last_s", [P, DEC_B, NG], F32)
        h_tmp = sb("h_tmp", [P, 2, DEC_B, NG], F32)
        t_all = sb("t_all", [P, L, NG, GC], F32)
        w_glu = sb("w_glu", [P, KS, DS], F32)
        y_chunk, z_in, yT = u_chunk, u_perm, e_end

        with ExitStack() as inputs:
            sb = lambda *args: inputs.enter_context(nc.sbuf_tensor(*args))
            ps = lambda *args: inputs.enter_context(nc.psum_tensor(*args))
            lam_rows = sb("lam_rows", [NG, 2, P], F32)
            b_1 = sb("b_1", [P, NG, GC], F32)
            b_2 = sb("b_2", [P, NG, GC], F32)
            bbar = sb("bbar", [P, 2, NG, GC], F32)
            c_rows = sb("c_rows", [P, 4, 2, P], F32)
            st_rows = sb("st_rows", [P, 2, 2, P], F32)
            lam = sb("lam", [P, 2, NG], F32)
            w = sb("w", [P, 16, NG], F32)
            turns = sb("turns", [P, NG], I32)
            pow_down = sb("pow_down", [P, 2, NG, 9], F32)
            w_12 = sb("w_12", [P, GB, 3, NS], F32)
            shift_id = sb("shift_id", [P, 2 * P], F32)
            ps_w = ps("ps_w", [P, 512], F32)
            ps_k = ps("ps_k", [P, 512], F32)
            ps_e = ps("ps_e", [P, 2, 512], F32)
            ps_x = ps("ps_x", [P, 2, 512], F32)
            loaded, c_loaded, glu_loaded = sem("ssm_loaded"), sem("c_loaded"), sem("glu_loaded")
            perm_done, u_written, u_back = sem("perm_done"), sem("u_written"), sem("u_back")
            lam_tr, lam_sb, exp_done, red_done, sin_done = sem("lam_tr"), sem("lam_sb"), sem("dt_exp"), sem("red_done"), sem("sin_done")
            rows_tr, rows_sb, consts_c = sem("rows_tr"), sem("rows_sb"), sem("consts_c")
            x_done, w_tr, w_sb, e_mm, e_sb = sem("x_done"), sem("w_tr"), sem("w_sb"), sem("e_mm"), sem("e_sb")
            k7_sb, shift_mm, shift_sb = sem("k7_sb"), sem("shift_mm"), sem("shift_sb")

            with nc.Block(no_gpsimd_drain=True) as block:

                @block.sync
                def _(sp):
                    for i, name in enumerate(("lambda_re", "lambda_im")):
                        for h in range(2):
                            sp.dma_start(lam_rows[:, i, h * NS:(h + 1) * NS], a[name][0]).then_inc(loaded, 16)
                    sp.wait_ge(perm_done, KS)
                    sp.dma_start(u_scr.rearrange("(k p) x -> p k x", p=P), u_perm[:, :, :, :].rearrange("p k s n -> p k (s n)")).then_inc(u_written, 16)
                    sp.wait_ge(u_written, 16)
                    for s in range(L):
                        sp.dma_start(u_chunk[GC * s:GC * s + GC, :, :],
                                     u_scr[:, s * NCH:(s + 1) * NCH].rearrange("(g c) n -> c g n", c=GC)).then_inc(u_back, 16)
                    sp.dma_start(w_glu[:, :, :], a["w_glu"][0].rearrange("(k p) n -> p k n", p=P)).then_inc(glu_loaded, 16)
                    sp.wait_ge(u_back, 16 * L)
                    sp.wait_ge(glu_loaded, 16)

                @block.scalar
                def _(act):
                    act.sem_inc(e_sb, 1)
                    with nc.allow_non_contiguous_dma(reason="runs of 64 bytes"):
                        for tile, names in ((b_1, ("b_re", "b_im")), (b_2, ("b_im", "b_re"))):
                            for h, name in enumerate(names):
                                act.dma_start(tile[h * NS:(h + 1) * NS, :, :], a[name][0].rearrange("g p c -> p g c")).then_inc(loaded, 16)
                    for i, names in enumerate((("c_re", "c_im"), ("c_im", "c_re"))):
                        for h, name in enumerate(names):
                            act.dma_start(c_rows[:, :, i, h * NS:(h + 1) * NS],
                                          a[name][0].rearrange("(t g) c p -> (g c) t p", t=4)).then_inc(c_loaded, 16)
                    for i, names in enumerate((("re", "im"), ("im", "re"))):
                        for h, name in enumerate(names):
                            act.dma_start(st_rows[:, :, i, h * NS:(h + 1) * NS],
                                          a["state_ssm_" + name][0].rearrange("(t b) g p -> (b g) t p", t=2)).then_inc(c_loaded, 16)
                    for k in range(KS):
                        act.copy(u_perm[:, k, :, :], m.uT[:, k, :].rearrange("p (n s) -> p s n", s=L)).then_inc(perm_done, 1)
                    act.activation(w[:, 0, :], m.log_dt, ACT.Exp).then_inc(exp_done, 1)
                    act.wait_ge(red_done, 1)
                    act.activation(w[:, 3, :], w[:, 1, :], ACT.Exp)
                    act.activation(w[:, 5, :], w[:, 4, :], ACT.Sin)
                    act.activation(w[:, 6, :], w[:, 4, :], ACT.Sin, scale=0.5).then_inc(sin_done, 1)

                    with act.Fori(0, N_GB) as i:
                        act.wait_ge(w_tr, i + 2)
                        blk = ps_w[:, :].rearrange("p (g x) -> p g x", g=GB)
                        act.wait_ge(e_mm, i + 1)
                        act.copy(w_12[:, :, 0:2, :].rearrange("p g a x -> p g (a x)"), blk)
                        act.copy(w_12[:, :, 2, :], blk[:, :, 0:NS]).then_inc(w_sb, 1)
                        act.wait_ge(e_mm, i + 2)
                        for half in range(2):
                            for g in range(2):
                                last = act.copy(e_end[:, :, :, bass.ds(i * GB + 2 * half + g, 1)].rearrange("p n w g -> p w (n g)"),
                                                ps_e[:, half, g * 2 * NCH:(g + 1) * 2 * NCH].rearrange("p (w n) -> p w n", w=2))
                        last.then_inc(e_sb, 1)
                    act.wait_ge(e_mm, N_GB + 1)
                    act.copy(t_all[:, L - 1, :, :].rearrange("p g c -> p (g c)"), ps_k[:, :]).then_inc(k7_sb, 1)
                    for i, t in enumerate(range(L - 1)):
                        act.wait_ge(shift_mm, i + 1)
                        act.copy(t_all[:, t, :, :].rearrange("p g c -> p (g c)"), ps_x[:, i % 2, :]).then_inc(shift_sb, 1)
                    act.drain()

                @block.gpsimd
                def _(pool):
                    pool.memset(sgn[0:NS, 0:1], -1.0)
                    pool.drain()
                    pool.memset(sgn[NS:P, 0:1], 1.0)
                    pool.drain()
                    pool.memset(shift_id[:, :], 0.0)
                    pool.drain()
                    pool.affine_select(out=shift_id[:, :], in_=shift_id[:, :], compare_op=ALU.not_equal, fill=1.0, base=0,
                                       pattern=[[-1, 2 * P]], channel_multiplier=1)
                    pool.drain()
                    pool.sem_inc(consts_c, 1)

                @block.vector
                def _(dve):
                    W = lambda i: w[:, i, :]
                    LR, LI = lam[:, 0, :], lam[:, 1, :]

                    def tt(out, x, y, op):
                        return dve.tensor_tensor(out, x, y, op)

                    dve.wait_ge(lam_tr, 1)
                    dve.tensor_copy(lam[:, :, :], ps_w[:, 0:2 * NG].rearrange("p (a g) -> p a g", a=2)).then_inc(lam_sb, 1)
                    dve.wait_ge(exp_done, 1)
                    dve.drain()
                    tt(W(1), LR, W(0), ALU.mult)
                    tt(W(2), LI, W(0), ALU.mult)
                    dve.drain()
                    dve.tensor_scalar(turns[:, :], W(2), float(1 / (2 * np.pi)), None, ALU.mult)
                    dve.drain()
                    dve.tensor_copy(W(7), turns[:, :])
                    dve.drain()
                    for part in (TWO_PI_A, TWO_PI_B, TWO_PI_C):
                        dve.scalar_tensor_tensor(W(2), W(7), -part, W(2), ALU.mult, ALU.add)
                        dve.drain()
                    dve.tensor_scalar(W(4), W(2), PI_IN, -PI_IN, ALU.min, ALU.max).then_inc(red_done, 1)
                    dve.wait_ge(sin_done, 1)
                    tt(W(6), W(6), W(6), ALU.mult)
                    dve.drain()
                    dve.tensor_scalar(W(6), W(6), -2.0, 1.0, ALU.mult, ALU.add)
                    dve.drain()
                    tt(W(6), W(6), W(3), ALU.mult)
                    tt(W(5), W(5), W(3), ALU.mult)
                    dve.drain()
                    dve.tensor_scalar(W(7), W(6), 1.0, None, ALU.subtract)
                    tt(W(8), LR, LR, ALU.mult)
                    tt(W(9), LI, LI, ALU.mult)
                    dve.drain()
                    tt(W(8), W(8), W(9), ALU.add)
                    tt(W(13), W(7), LR, ALU.mult)
                    tt(W(10), W(5), LI, ALU.mult)
                    tt(W(11), W(5), LR, ALU.mult)
                    tt(W(12), W(7), LI, ALU.mult)
                    dve.drain()
                    dve.reciprocal(W(8), W(8))
                    tt(W(9), W(13), W(10), ALU.add)
                    tt(W(11), W(11), W(12), ALU.subtract)
                    dve.wait_ge(consts_c, 1)
                    dve.drain()
                    tt(W(9), W(9), W(8), ALU.mult)
                    tt(W(11), W(11), W(8), ALU.mult)
                    dve.tensor_scalar(W(5), W(5), sgn[:, 0:1], None, ALU.mult)
                    dve.drain()
                    dve.tensor_scalar(W(11), W(11), sgn[:, 0:1], None, ALU.mult)
                    re, im = (lambda j: pow_up[:, 0, :, j]), (lambda j: pow_up[:, 1, :, j])
                    dve.memset(pow_up[:, 0, :, 0:1], 1.0)
                    dve.memset(pow_up[:, 1, :, 0:1], 0.0)
                    dve.tensor_copy(re(1), W(6))
                    dve.tensor_copy(im(1), W(5))
                    dve.drain()
                    for j in range(2, 9):
                        tt(W(12), W(6), re(j - 1), ALU.mult)
                        tt(W(13), W(5), im(j - 1), ALU.mult)
                        tt(W(14), W(6), im(j - 1), ALU.mult)
                        tt(W(15), W(5), re(j - 1), ALU.mult)
                        dve.drain()
                        tt(re(j), W(12), W(13), ALU.subtract)
                        tt(im(j), W(14), W(15), ALU.add)
                        dve.drain()
                    for j in range(9):
                        dve.tensor_copy(pow_down[:, :, :, 8 - j], pow_up[:, :, :, j])
                    for i in range(2):
                        dve.tensor_copy(step_ab[:, 0, i, :], re(8))
                    dve.tensor_copy(step_ab[:, 1, 0, :], im(8))
                    dve.tensor_scalar(step_ab[:, 1, 1, :], im(8), -1.0, None, ALU.mult)
                    dve.wait_ge(loaded, 16 * 8)
                    f_re = W(9).unsqueeze(2).to_broadcast((P, NG, GC))
                    f_im = W(11).unsqueeze(2).to_broadcast((P, NG, GC))
                    t0 = t_all[:, 0, :, :]
                    t1 = t_all[:, 1, :, :]
                    tt(bbar[:, 0], b_1[:, :, :], f_re, ALU.mult)
                    tt(bbar[:, 1], b_2[:, :, :], f_re, ALU.mult)
                    tt(t0, b_2[:, :, :], f_im, ALU.mult)
                    tt(t1, b_1[:, :, :], f_im, ALU.mult)
                    dve.drain()
                    tt(bbar[:, 0], bbar[:, 0], t0, ALU.add)
                    tt(bbar[:, 1], bbar[:, 1], t1, ALU.subtract)
                    dve.tensor_scalar(sgn[:, 1:2], sgn[:, 0:1], -1.0, None, ALU.mult)
                    dve.drain()
                    for i in range(2):
                        dve.wait_ge(rows_tr, i + 1)
                        dve.tensor_scalar(c_12[:, i, :, :].rearrange("p g c -> p (g c)"), ps_x[:, i, :], sgn[:, 1:2], None, ALU.mult).then_inc(rows_sb, 1)
                    dve.wait_ge(rows_tr, 3)
                    dve.tensor_copy(h_start[:, NC_P:NCH, :, :].rearrange("p b w g -> p w b g"),
                                    ps_x[:, 0, :].rearrange("p (w b g) -> p w b g", w=2, b=DEC_B)).then_inc(rows_sb, 1)

                    with dve.Fori(0, N_GB) as i:
                        dve.wait_ge(w_tr, i + 1)
                        dve.wait_ge(e_mm, i + 1)
                        gs = bass.ds(i * GB, GB)
                        xs = [x_pow[:, j, :, :].rearrange("p g (s c) -> p g s c", s=L) for j in range(2)]
                        for j in range(2):
                            tt(xs[j], pow_down[:, j, gs, 1:9].unsqueeze(3).to_broadcast((P, GB, L, GC)),
                               bbar[:, j, gs, :].unsqueeze(2).to_broadcast((P, GB, L, GC)), ALU.mult)
                        dve.drain()
                        tt(x_pow[:, 0], x_pow[:, 0], x_pow[:, 1], ALU.add).then_inc(x_done, 1)

                @block.tensor
                def _(pe):
                    for done in (w_tr, e_mm):
                        pe.sem_inc(done, 1)
                    pe.wait_ge(loaded, 16 * 8)
                    for i in range(2):
                        last = pe.transpose(ps_w[:, i * NG:(i + 1) * NG], lam_rows[:, i, :], m.ident[0:NG, 0:NG])
                    last.then_inc(lam_tr, 1)
                    pe.wait_ge(c_loaded, 16 * 8)
                    for i in range(2):
                        for t in range(4):
                            last = pe.transpose(ps_x[:, i, t * P:(t + 1) * P], c_rows[:, t, i, :], m.ident[:, :])
                        last.then_inc(rows_tr, 1)
                    pe.wait_ge(rows_sb, 1)
                    for i in range(2):
                        for t in range(2):
                            last = pe.transpose(ps_x[:, 0, (2 * i + t) * P:(2 * i + t + 1) * P], st_rows[:, t, i, :], m.ident[:, :])
                    last.then_inc(rows_tr, 1)
                    pe.wait_ge(rows_sb, 3)
                    pe.wait_ge(lam_sb, 1)
                    pe.wait_ge(u_back, 16 * L)
                    with pe.Fori(0, N_GB) as i:
                        pe.wait_ge(x_done, i + 1)
                        for g in range(GB):
                            pe.transpose(ps_w[:, g * P:(g + 1) * P], x_pow[:, 0, g, :], m.ident[:, :])
                        for g in range(GB):
                            last = pe.matmul(ps_k[:, bass.ds(i * GB * GC + g * GC, GC)], x_pow[:, 0, g, :],
                                             c_12[:, 0, bass.ds(i * GB + g, 1), :].rearrange("p a c -> p (a c)"), start=True, stop=True, skip_group_check=True)
                        last.then_inc(w_tr, 1)
                        pe.wait_ge(w_sb, i + 1)
                        pe.wait_ge(e_sb, i + 1)
                        for g in range(GB):
                            for k in range(2):
                                at = (2 * (g % 2) + k) * NCH
                                last = pe.matmul(ps_e[:, g // 2, at:at + NCH], w_12[:, g, k:k + 2, :].rearrange("p a x -> p (a x)"),
                                                 u_chunk[:, bass.ds(i * GB + g, 1), :].rearrange("p a n -> p (a n)"), start=True, stop=True)
                        last.then_inc(e_mm, 1)
                    pe.wait_ge(k7_sb, 1)
                    pe.wait_ge(consts_c, 1)
                    for i, t in enumerate(range(L - 1)):
                        if i >= 2:
                            pe.wait_ge(shift_sb, i - 1)
                        at = GC * (L - 1 - t)
                        pe.matmul(ps_x[:, i % 2, :], shift_id[:, at:at + P], t_all[:, L - 1, :, :].rearrange("p g c -> p (g c)"),
                                  start=True, stop=True).then_inc(shift_mm, 1)

        end_stage(nc, m)

        def recurrence(pool, part):
            tt = pool.tensor_tensor
            a8, b8 = step_ab[:, 0, :, :], step_ab[:, 1, :, :]
            t_a, t_b = h_tmp[:, :, 0, :], h_tmp[:, :, 1, :]

            def step(now, e, nxt):
                tt(t_a, now, a8, ALU.mult)
                tt(t_b[:, 0, :], now[:, 1, :], b8[:, 0, :], ALU.mult)
                tt(t_b[:, 1, :], now[:, 0, :], b8[:, 1, :], ALU.mult)
                pool.drain()
                tt(t_a, t_a, t_b, ALU.add)
                pool.drain()
                tt(nxt, t_a, e, ALU.add)
                pool.drain()

            if part == "start":
                pool.memset(h_start[:, 0, :, :], 0.0)
                pool.drain()
            elif part == "end":
                step(h_start[:, NC_P - 1], e_end[:, NC_P - 1], h_last[:, :, :])
                full = lambda x: x.unsqueeze(1).to_broadcast((P, DEC_B, NG))
                tt(h_tmp[:, 0], h_start[:, NC_P:NCH, 0, :], full(step_ab[:, 0, 0, :]), ALU.mult)
                tt(h_tmp[:, 1], h_start[:, NC_P:NCH, 1, :], full(step_ab[:, 1, 0, :]), ALU.mult)
                pool.drain()
                tt(h_tmp[:, 0], h_tmp[:, 0], h_tmp[:, 1], ALU.add)
                pool.drain()
                tt(h_last_s[:, :, :], h_tmp[:, 0], e_end[:, NC_P:NCH, 0, :], ALU.add)
                pool.drain()
            else:
                first, count = part
                with pool.Fori(0, count) as n:
                    at = lambda tile, k: tile[:, bass.ds(first + n + k, 1), :, :].rearrange("p n w g -> p (n w) g")
                    step(at(h_start, 0), at(e_end, 0), at(h_start, 1))

        prompt_attention(nc, a, o, m, recurrence)
        end_stage(nc, m)

        sb = lambda *args: scope.enter_context(nc.sbuf_tensor(*args))
        ps = lambda *args: scope.enter_context(nc.psum_tensor(*args))
        t_blk = sb("t_blk", [P, 2, GB, P], F32)
        v_blk = sb("v_blk", [P, GB, P], F32)
        st_out = sb("st_out", [P, 3, P], F32)
        ps_w = ps("ps_w2", [P, 512], F32)
        ps_e = ps("ps_e2", [P, 2, 512], F32)
        ps_x = ps("ps_x2", [P, 2, 512], F32)
        v_built, t_staged, y_mm, y_sb = sem("v_built"), sem("t_staged"), sem("y_mm"), sem("y_sb")
        fin_tr, fin_sb, fin_out = sem("fin_tr"), sem("fin_sb"), sem("fin_out")
        y_written, y_back, skip_done, z_done = sem("y_written"), sem("y_back"), sem("skip_done"), sem("z_done")
        glu_mm, gate_done, glu_done = sem("glu_mm"), sem("gate_done"), sem("glu_done")

        with nc.Block(no_gpsimd_drain=True) as block:

            @block.sync
            def _(sp):
                sp.wait_ge(fin_sb, 1)
                sp.dma_start(o["ssm_re_prompt"][0, 0], st_out[0:NG, 0, 0:NS]).then_inc(fin_out, 16)
                sp.dma_start(o["ssm_im_prompt"][0, 0], st_out[0:NG, 0, NS:P]).then_inc(fin_out, 16)
                for i, name in enumerate(("ssm_re_sample", "ssm_im_sample")):
                    sp.dma_start(o[name][0].rearrange("(t b) g p -> (b g) t p", t=2), st_out[:, 1:3, i * NS:(i + 1) * NS]).then_inc(fin_out, 16)
                sp.wait_ge(y_sb, N_GB + 1)
                for t in range(L):
                    sp.dma_start(y_scr[:, t * NCH:(t + 1) * NCH].rearrange("(g c) n -> c g n", c=GC),
                                 y_chunk[GC * t:GC * t + GC, :, :]).then_inc(y_written, 16)
                sp.wait_ge(y_written, 16 * L)
                sp.dma_start(yT[:, :, :, :].rearrange("p n w g -> p (n w g)")[:, 0:KS * T].rearrange("p (k x) -> p k x", k=KS),
                             y_scr.rearrange("(k p) x -> p k x", p=P)).then_inc(y_back, 16)
                sp.wait_ge(fin_out, 16 * 4)

            @block.scalar
            def _(act):
                with act.Fori(0, N_GB // 2) as i:
                    for b in range(2):
                        act.wait_ge(y_mm, 2 * i + b + 1)
                        act.copy(t_blk[:, b, :, :].rearrange("p g (t c) -> p g t c", t=L),
                                 t_all[:, :, bass.ds((2 * i + b) * GB, GB), :].rearrange("p t g c -> p g t c")).then_inc(t_staged, 1)
                act.wait_ge(fin_tr, 1)
                act.copy(st_out[0:NG, 0, :], ps_x[0:NG, 1, 0:P])
                act.copy(st_out[:, 1:3, :], ps_x[:, 1, P:3 * P].rearrange("p (a x) -> p a x", a=2)).then_inc(fin_sb, 1)
                for k in range(KS):
                    act.wait_ge(skip_done, k + 1)
                    act.activation(z_in[:, k, :, :].rearrange("p s n -> p (s n)"), z_in[:, k, :, :].rearrange("p s n -> p (s n)"),
                                   ACT.Gelu_apprx_tanh).then_inc(z_done, 1)
                for c in range(KS):
                    act.wait_ge(glu_mm, c + 1)
                    bias = m.columns[:, m.col["b_glu"] + c:m.col["b_glu"] + c + 1]
                    act.activation(m.mixT[:, KA + c, 0:SEQ], (ps_e, ps_x)[c % 2][:, 0, :], ACT.Sigmoid, bias=bias)
                    act.activation(m.mixT[:, KA + c, SEQ:T], (ps_e, ps_x)[c % 2][:, 1, 0:T_S], ACT.Sigmoid, bias=bias).then_inc(gate_done, 1)

            @block.vector
            def _(dve):
                tt = dve.tensor_tensor
                dve.sem_inc(y_sb, 1)
                with dve.Fori(0, N_GB) as i:
                    gs = bass.ds(i * GB, GB)
                    dve.wait_ge(y_mm, i + 1)
                    vs = v_blk[:, :, :].rearrange("p g (t c) -> p g t c", t=L)
                    xv = x_pow[:, 1, :, :].rearrange("p g (t c) -> p g t c", t=L)
                    for j, dst in ((0, vs), (1, xv)):
                        tt(dst, pow_up[:, j, gs, 1:9].unsqueeze(3).to_broadcast((P, GB, L, GC)),
                           c_12[:, j, gs, :].unsqueeze(2).to_broadcast((P, GB, L, GC)), ALU.mult)
                    dve.drain()
                    tt(v_blk[:, :, :], v_blk[:, :, :], x_pow[:, 1], ALU.add).then_inc(v_built, 1)
                    dve.wait_ge(y_mm, i + 2)
                    dve.tensor_copy(y_chunk[:, gs, :], ps_w[:, 0:GB * NCH].rearrange("p (g n) -> p g n", g=GB)).then_inc(y_sb, 1)
                dve.wait_ge(y_back, 16)
                y_flat = yT[:, :, :, :].rearrange("p n w g -> p (n w g)")
                for k in range(KS):
                    dve.scalar_tensor_tensor(z_in[:, k, :, :].rearrange("p s n -> p (s n)").rearrange("p (n s) -> p s n", s=L),
                                             m.uT[:, k, :].rearrange("p (n s) -> p s n", s=L),
                                             m.columns[:, m.col["d_skip"] + k:m.col["d_skip"] + k + 1],
                                             y_flat[:, k * T:(k + 1) * T].rearrange("p (s n) -> p s n", s=L), ALU.mult, ALU.add).then_inc(skip_done, 1)
                for c in range(KS):
                    dve.wait_ge(gate_done, c + 1)
                    tt(m.mixT[:, KA + c, :], m.mixT[:, KA + c, :], z_in[:, c, :, :].rearrange("p s n -> p (s n)"), ALU.mult).then_inc(glu_done, 1)

            @block.tensor
            def _(pe):
                pe.sem_inc(y_mm, 1)
                pe.transpose(ps_x[0:NG, 1, 0:P], h_last[:, 0, :], m.ident[:, :])
                for i in range(2):
                    last = pe.transpose(ps_x[:, 1, (1 + i) * P:(2 + i) * P],
                                        h_last_s[:, 4 * i:4 * i + 4, :].rearrange("p b g -> p (b g)"), m.ident[:, :])
                last.then_inc(fin_tr, 1)
                with pe.Fori(0, N_GB // 2) as i:
                    for b in range(2):
                        n = 2 * i + b
                        pe.wait_ge(t_staged, n + 1)
                        pe.wait_ge(v_built, n + 1)
                        pe.wait_ge(y_sb, n + 1)
                        for g in range(GB):
                            out = ps_w[:, g * NCH:(g + 1) * NCH]
                            grp = bass.ds(n * GB + g, 1)
                            pe.matmul(out, t_blk[:, b, g, :], u_chunk[:, grp, :].rearrange("p a n -> p (a n)"), start=True, stop=False)
                            last = pe.matmul(out, v_blk[:, g, :], h_start[:, :, 0, grp].rearrange("p n g -> p (n g)"), start=False, stop=True)
                        last.then_inc(y_mm, 1)
                pe.wait_ge(z_done, KS)
                pe.wait_ge(fin_sb, 1)
                for c in range(KS):
                    if c >= 2:
                        pe.wait_ge(gate_done, c - 1)
                    bank = (ps_e, ps_x)[c % 2]
                    for part, (lo, n) in enumerate(((0, SEQ), (SEQ, T_S))):
                        for k in range(KS):
                            last = pe.matmul(bank[:, part, 0:n], w_glu[:, k, c * P:(c + 1) * P],
                                             z_in[:, k, :, :].rearrange("p s n -> p (s n)")[:, lo:lo + n], start=(k == 0), stop=(k == KS - 1))
                    last.then_inc(glu_mm, 1)


RING = 8
RING_V = 2 * RING
IDS = 16
N_RUN = NPG // RING
GRP = 4
N_GRP = NPG // GRP
PAST = NPG * PAGE
ROWS = P


def sample_attention(nc, a, o, m):
    sem = m.sem
    table = a["page_table"]
    logf_pages = a["cache_logf"][0].rearrange("n k h -> n (k h)")
    bias_scr = nc.dram_tensor("bias_scr", (DEC_B, NH, NPG, PAGE), F32, kind="Internal").ap()
    with ExitStack() as scope:
        sb = lambda *args: scope.enter_context(nc.sbuf_tensor(*args))
        ps = lambda *args: scope.enter_context(nc.psum_tensor(*args))
        k_ring = sb("k_ring", [P, RING, DA], F32)
        v_ring = sb("v_ring", [P, RING, DA], F32)
        k_places = [k_ring[:, i, :] for i in range(RING)]
        v_places = [v_ring[:, i, :] for i in range(RING)] + [m.v[:, t, :] for t in range(PT)] + [m.kT[:, j, 0:SEQ] for j in range(HP)]
        page_row = sb("page_row", [1, DEC_B * NPG], I32)
        page_col = sb("page_col", [P, 2, 1], I32)
        seq_after = sb("seq_after", [P, P], F32)
        after = sb("after", [P, 2, NH], F32)
        bias = sb("bias", [ROWS, PAST], F32)
        head_of = sb("head_of", [NH, HP, 4, DEC_S], F32)
        query_of = sb("query_of", [DEC_S, HP, 4, DEC_S], F32)
        mask_q = sb("mask_q", [DEC_S, DEC_B, T_S], F32)
        neg_cn = sb("neg_cn", [T_S, NH], F32)
        neg_cnT = sb("neg_cnT", [NH, T_S], F32)
        bias_new = sb("bias_new", [ROWS, DEC_B, T_S], F32)
        q_rows = sb("q_rows", [P, DEC_B, HP, 4, DEC_S], F32)
        q_now = sb("q_now", [P, HP, 4 * DEC_S], F32)
        kT_grp = sb("kT_grp", [P, 2, HP, GRP * PAGE], F32)
        scores = sb("scores", [ROWS, 2, PAST + T_S], F32)
        probs = sb("probs_s", [ROWS, PAST + T_S], F32)
        g_max = sb("g_max", [ROWS, N_GRP + 1], F32)
        row = sb("row", [ROWS, 2, 4], F32)
        pT = m.uT[:, :, :].rearrange("p a n -> p (a n)")[:, 0:2 * GRP * ROWS].rearrange("p (g n) -> p g n", g=2)
        pT_new = sb("pT_new", [T_S, ROWS], F32)
        o_rows = sb("o_rows", [ROWS, P], F32)
        ps_kT = ps("ps_kT", [P, GRP, 512], F32)
        ps_sc = ps("ps_sc", [P, 2, 512], F32)
        ps_new = ps("ps_new", [P, 512], F32)
        ps_out = ps("ps_out", [P, 512], F32)
        ps_pT = ps_kT[:, 0:2, :]
        lf_page = scores[:, 0, 0:2 * PAGE * NH].rearrange("p (t x) -> p t x", t=2)
        suffix = probs[:, 0:2 * PAGE * NH].rearrange("p (t h k) -> p t h k", t=2, h=NH)

        table_in, lf_in = sem("table_in"), sem("lf_in")
        k_in = [sem(f"k_in{i}") for i in range(RING)]
        v_in = [sem(f"v_in{i}") for i in range(RING_V)]
        masks_done, tot_done, after_mm, suffix_done, bias_written, bias_in, bias_used = (
            sem(x) for x in ("masks_done", "tot_done", "after_mm", "suffix_done", "bias_written", "bias_in", "bias_used"))
        cn_mm, cn_sb, cnT_mm, cnT_sb, bn_mm, q_done = (sem(x) for x in ("cn_mm", "cn_sb", "cnT_mm", "cnT_sb", "bn_mm", "q_done"))
        q_ready = sem("q_ready")
        kT_mm, kT_act, kT_dve, sc_mm, sc_taken = sem("kT_mm"), sem("kT_act"), sem("kT_dve"), sem("sc_mm"), sem("sc_taken")
        new_mm, new_taken, max_neg, exp_done = sem("new_mm"), sem("new_taken"), sem("max_neg"), sem("exp_done")
        pT_mm, pT_even, pT_odd, pTn_mm, pTn_sb = sem("pT_mm"), sem("pT_even"), sem("pT_odd"), sem("pTn_mm"), sem("pTn_sb")
        v_used, out_mm, o_rows_done, oT_mm, oT_taken = sem("v_used"), sem("out_mm"), sem("o_rows_done"), sem("oT_mm_s"), sem("oT_taken")

        with nc.Block(no_gpsimd_drain=True) as block:

            @block.sync
            def _(sp):
                sp.dma_start(page_row[:, :], table.rearrange("b p -> (b p)").unsqueeze(0)).then_inc(table_in, 16)
                with nc.allow_non_contiguous_dma(reason="256 indices"):
                    sp.dma_start(page_col[:, :, :], table.rearrange("(t b) p -> (b p) t", t=2).unsqueeze(2)).then_inc(table_in, 16)
                sp.wait_ge(table_in, 32)

                def pages(cache, ring, arrived, used, b):
                    with sp.Fori(0, NPG // IDS) as r:
                        for i in range(IDS):
                            n = b * NPG + r * IDS + i
                            if i == 0:
                                _, ids = nc.values_load_multi_w_load_instructions(
                                    page_row[0:1, bass.ds(n, IDS)], engines=(mybir.EngineType.SP,), min_val=0, max_val=N_POOL - 1)
                            sp.wait_ge(used, n + 1)
                            sp.dma_start(ring[i % len(ring)], cache[0, bass.ds(ids[i], 1)].rearrange("n k h d -> (n k) (h d)")).then_inc(arrived[i % len(ring)], 16)

                def row_bias(b):
                    sp.wait_ge(bias_used, b)
                    for j in range(HP):
                        src = bias_scr[bass.ds(b, 1), 2 * j:2 * j + 2].rearrange("b h g k -> (b h) (g k)")
                        sp.dma_start(bias[32 * j:32 * j + 2 * DEC_S, :],
                                     src.unsqueeze(1).to_broadcast((2, DEC_S, PAST))).then_inc(bias_in, 16)

                sp.wait_ge(suffix_done, 1)
                for b in range(DEC_B):
                    t, at = b // 4, (b % 4) * NPG
                    sp.dma_start(bias_scr[b].rearrange("h g k -> g h k"), suffix[at:at + NPG, t, :, :]).then_inc(bias_written, 16)
                sp.wait_ge(bias_written, 16 * DEC_B)
                row_bias(0)
                pages(a["cache_k"], k_places, k_in, kT_mm, 0)
                with sp.Fori(0, DEC_B - 1) as b:
                    row_bias(b + 1)
                    pages(a["cache_k"], k_places, k_in, kT_mm, b + 1)
                    pages(a["cache_v"], v_places, v_in, v_used, b)
                pages(a["cache_v"], v_places, v_in, v_used, DEC_B - 1)

            @block.gpsimd
            def _(pool):
                for tile, value in ((seq_after[:, :], 1.0), (q_rows[:, :, :, :, :], 0.0), (bias[:, :], 0.0),
                                    (head_of[:, :, :, :], 0.0), (query_of[:, :, :, :], 0.0), (mask_q[:, :, :], 0.0)):
                    pool.memset(tile, value)
                pool.drain()

                def select(view, op, fill, base, pattern, cm):
                    pool.affine_select(out=view, in_=view, compare_op=op, fill=fill, base=base, pattern=pattern, channel_multiplier=cm)

                select(seq_after[:, :], ALU.is_gt, 0.0, 0, [[-1, P]], 1)
                select(head_of[:, :, 0:2, :], ALU.not_equal, 1.0, 0, [[-2, HP], [-1, 2], [0, DEC_S]], 1)
                select(query_of[:, :, :, :].rearrange("a j e q -> a (j e) q"), ALU.not_equal, 1.0, 0, [[0, 4 * HP], [-1, DEC_S]], 1)
                select(mask_q[:, :, :], ALU.is_ge, MASKED, 0, [[-DEC_S, DEC_B], [1, T_S]], 0)
                pool.drain()
                select(seq_after[:, :].rearrange("j (b k) -> j b k", k=NPG), ALU.is_gt, 0.0, NPG, [[NPG, P // NPG], [0, NPG]], -1)
                select(mask_q[:, :, :], ALU.is_ge, MASKED, 0, [[DEC_S, DEC_B], [-1, T_S]], 1)
                pool.drain()
                pool.sem_inc(masks_done, 1)
                pool.wait_ge(table_in, 32)
                for t in range(2):
                    pool.indirect_dma_start(lf_page[:, t, :], None, logf_pages, bass.IndirectOffsetOnAxis(ap=page_col[:, t, :], axis=0),
                                            bounds_check=N_POOL - 1).then_inc(lf_in, 16)
                pool.wait_ge(q_done, 1)
                with pool.Fori(0, DEC_B) as b:
                    pool.wait_ge(new_mm, b + 1)
                    pool.tensor_copy(q_now[:, :, :], q_rows[:, bass.ds(b, 1), :, :, :].rearrange("p b j e q -> p (b j) (e q)")).then_inc(q_ready, 1)

            ACT_PAGES = (0, 1, 3)

            def kT_copy(eng, copy, done, b, r, i):
                n = b * NPG + r * RING + i
                eng.wait_ge(kT_mm, n + 1 + RING)
                if i % GRP == (0 if done is kT_act else 2):
                    eng.wait_ge(sc_mm, b * N_GRP + r * (RING // GRP) + i // GRP + 1)
                g, at = (i // GRP) % 2, (i % GRP) * PAGE
                copy(kT_grp[:, g, :, at:at + PAGE], ps_kT[:, i % GRP, :].rearrange("p (a n) -> p a n", a=HP)).then_inc(done, 1)

            def pT_copy(eng, copy, parity, done, b, r, g):
                eng.wait_ge(pT_mm, b * N_GRP + r * (RING // GRP) + g + 1)
                eng.wait_ge(v_used, b * NPG + r * RING + g * GRP + RING_V - GRP)
                copy(pT[:, parity, :], ps_pT[:, parity, :]).then_inc(done, 1)

            @block.scalar
            def _(act):
                act.sem_inc(kT_act, len(ACT_PAGES))
                act.sem_inc(pT_even, 1)
                act.wait_ge(cnT_mm, 1)
                act.copy(neg_cnT[:, :], ps_new[0:NH, 64:64 + T_S]).then_inc(cnT_sb, 1)

                def k_copies(b):
                    with act.Fori(0, N_RUN) as r:
                        for i in range(RING):
                            if i % GRP in ACT_PAGES:
                                kT_copy(act, act.copy, kT_act, b, r, i)

                def exps(b, h):
                    act.wait_ge(max_neg, b + 1)
                    act.wait_ge(out_mm, b)
                    act.activation(probs[:, :], scores[:, h, :], ACT.Exp, bias=row[:, h, 1:2], accum_out=row[:, h, 2:3]).then_inc(exp_done, 1)

                def p_copies(b):
                    act.wait_ge(pTn_mm, b + 1)
                    act.copy(pT_new[:, :], ps_new[0:T_S, 128:256]).then_inc(pTn_sb, 1)
                    with act.Fori(0, N_RUN) as r:
                        for g in range(0, RING // GRP, 2):
                            pT_copy(act, act.copy, 0, pT_even, b, r, g)

                def turn(b, h):
                    k_copies(b + 1)
                    p_copies(b)
                    exps(b + 1, 1 - h)

                k_copies(0)
                exps(0, 0)
                turn(0, 0)
                with act.Fori(0, DEC_B // 2 - 1) as c:
                    for h in (1, 0):
                        turn(c * 2 + (2 - h), h)
                p_copies(DEC_B - 1)

            @block.vector
            def _(dve):
                for done in (kT_dve, pT_odd, oT_taken):
                    dve.sem_inc(done, 1)
                dve.wait_ge(masks_done, 1)
                q_new = m.qT[:, :, SEQ:T].rearrange("p a (b i) -> p b a i", i=DEC_S)
                dve.tensor_copy(q_rows[0:HD, :, :, 0, :], q_new[0:HD])
                dve.tensor_copy(q_rows[HD:P, :, :, 1, :], q_new[HD:P]).then_inc(q_done, 1)
                dve.wait_ge(cn_mm, 1)
                dve.tensor_scalar(neg_cn[:, :], ps_new[0:T_S, 0:NH], -1.0, None, ALU.mult).then_inc(cn_sb, 1)
                dve.wait_ge(bn_mm, 1)
                dve.tensor_copy(bias_new[:, :, :].rearrange("p b t -> p (b t)"), ps_sc[:, 0, :])
                dve.wait_ge(lf_in, 32)
                heads = lf_page.rearrange("p t (k h) -> p t h k", h=NH)
                for t in range(2):
                    for h in range(NH):
                        dve.tensor_tensor_scan(suffix[:, t, h, :], m.ones[:, :], heads[:, t, h, :], 0.0, ALU.mult, ALU.add)
                dve.drain()
                dve.tensor_copy(after[:, :, :], suffix[:, :, :, PAGE - 1]).then_inc(tot_done, 1)
                dve.wait_ge(after_mm, 1)
                dve.tensor_tensor(after[:, :, :], after[:, :, :], ps_new[:, 16:32].rearrange("p (t h) -> p t h", t=2), ALU.add)
                dve.drain()
                for t in range(2):
                    for h in range(NH):
                        last = dve.tensor_scalar(suffix[:, t, h, :], suffix[:, t, h, :], -1.0, after[:, t, h:h + 1], ALU.mult, ALU.add)
                last.then_inc(suffix_done, 1)
                dve.wait_ge(bias_written, 16 * DEC_B)
                dve.sem_inc(sc_taken, 2)

                def k_copies(b, h):
                    with dve.Fori(0, N_RUN) as r:
                        for g in range(RING // GRP):
                            kT_copy(dve, dve.tensor_copy, kT_dve, b, r, g * GRP + 2)
                            if g:
                                group(b, h, r, g - 1)
                        group(b, h, r, RING // GRP - 1)

                def group(b, h, r, g):
                    at = r * RING * PAGE + g * GRP * PAGE
                    if g == 0:
                        dve.wait_ge(bias_in, 16 * HP * (b + 1))
                    dve.wait_ge(sc_mm, b * N_GRP + r * (RING // GRP) + g + 3)
                    cols_ = bass.ds(at, GRP * PAGE)
                    dve.tensor_tensor(scores[:, h, cols_], ps_sc[:, g % 2, :], bias[:, cols_], ALU.add).then_inc(sc_taken, 1)
                    dve.drain()
                    dve.tensor_reduce(g_max[:, bass.ds(r * (RING // GRP) + g, 1)], scores[:, h, cols_], AX.X, ALU.max)

                def maximum(b, h):
                    dve.wait_ge(new_mm, b + 2)
                    dve.tensor_tensor(scores[:, h, PAST:PAST + T_S], ps_new[:, 64:64 + T_S], bias_new[:, bass.ds(b, 1), :].rearrange("p b t -> p (b t)"),
                                      ALU.add).then_inc(new_taken, 1)
                    dve.drain()
                    dve.tensor_reduce(g_max[:, N_GRP:N_GRP + 1], scores[:, h, PAST:PAST + T_S], AX.X, ALU.max)
                    dve.drain()
                    dve.sem_inc(bias_used, 1)
                    dve.tensor_reduce(row[:, h, 0:1], g_max[:, :], AX.X, ALU.max)
                    dve.drain()
                    dve.tensor_scalar(row[:, h, 1:2], row[:, h, 0:1], -1.0, None, ALU.mult).then_inc(max_neg, 1)

                def p_copies(b):
                    with dve.Fori(0, N_RUN) as r:
                        for g in range(1, RING // GRP, 2):
                            pT_copy(dve, dve.tensor_copy, 1, pT_odd, b, r, g)

                def output(b, h):
                    dve.wait_ge(exp_done, b + 1)
                    dve.reciprocal(row[:, h, 3:4], row[:, h, 2:3])
                    dve.drain()
                    dve.wait_ge(out_mm, b + 1)
                    dve.tensor_scalar(o_rows[:, :], ps_out[:, 0:P], row[:, h, 3:4], None, ALU.mult).then_inc(o_rows_done, 1)
                    dve.wait_ge(oT_mm, b + 1)
                    oT = ps_new[:, 256:256 + ROWS].rearrange("p (a e q) -> p a e q", a=HP, e=4)
                    for e in range(2):
                        rs = slice(e * HD, e * HD + HD)
                        last = dve.tensor_copy(m.mixT[rs, 0:HP, bass.ds(SEQ + b * DEC_S, DEC_S)], oT[rs, :, e, :])
                    last.then_inc(oT_taken, 1)

                def turn(b, h):
                    k_copies(b + 1, 1 - h)
                    maximum(b + 1, 1 - h)
                    p_copies(b)
                    output(b, h)

                k_copies(0, 0)
                maximum(0, 0)
                turn(0, 0)
                with dve.Fori(0, DEC_B // 2 - 1) as c:
                    for h in (1, 0):
                        turn(c * 2 + (2 - h), h)
                p_copies(DEC_B - 1)
                output(DEC_B - 1, 1)

            @block.tensor
            def _(pe):
                pe.sem_inc(kT_mm, RING)
                pe.sem_inc(v_used, RING_V)
                pe.sem_inc(sc_mm, 2)
                pe.sem_inc(new_mm, 1)
                pe.matmul(ps_new[0:T_S, 0:NH], m.tri_seq[:, :], m.logf[0:T_S, PT, :], start=True, stop=True).then_inc(cn_mm, 1)
                pe.wait_ge(cn_sb, 1)
                pe.transpose(ps_new[0:NH, 64:64 + T_S], neg_cn[:, :], m.ident[0:T_S, 0:T_S]).then_inc(cnT_mm, 1)
                pe.wait_ge(cnT_sb, 1)
                pe.wait_ge(masks_done, 1)
                flat = lambda x: x.rearrange("a j e q -> a (j e q)")
                pe.matmul(ps_sc[:, 0, :], flat(query_of[:, :, :, :]), mask_q[:, :, :].rearrange("q b t -> q (b t)"), start=True, stop=False)
                pe.matmul(ps_sc[:, 0, :], flat(head_of[:, :, :, :]), neg_cnT[:, :].unsqueeze(1).to_broadcast((NH, DEC_B, T_S)),
                          start=False, stop=True).then_inc(bn_mm, 1)
                pe.wait_ge(tot_done, 1)
                for t in range(2):
                    last = pe.matmul(ps_new[:, 16 + t * NH:16 + (t + 1) * NH], seq_after[:, :], after[:, t, :], start=True, stop=True)
                last.then_inc(after_mm, 1)
                def k_pages(b):
                    with pe.Fori(0, N_RUN) as r:
                        def turn(i):
                            pe.wait_ge(k_in[i], 16 * (b * N_RUN + r + 1))
                            group_no = b * N_GRP + r * (RING // GRP) + i // GRP
                            if i % GRP in ACT_PAGES:
                                pe.wait_ge(kT_act, group_no * len(ACT_PAGES) + ACT_PAGES.index(i % GRP) + 1)
                            else:
                                pe.wait_ge(kT_dve, group_no + 1)
                            for j in range(HP):
                                last = pe.transpose(ps_kT[:, i % GRP, j * P:(j + 1) * P], k_ring[:, i, j * P:(j + 1) * P], m.ident[:, :])
                            last.then_inc(kT_mm, 1)

                        def group(g):
                            pe.wait_ge(q_ready, b + 1)
                            pe.wait_ge(sc_taken, b * N_GRP + r * (RING // GRP) + g + 1)
                            group_no = b * N_GRP + r * (RING // GRP) + g
                            pe.wait_ge(kT_act, group_no * len(ACT_PAGES) + 2 * len(ACT_PAGES))
                            pe.wait_ge(kT_dve, group_no + 2)
                            for j in range(HP):
                                last = pe.matmul(ps_sc[32 * j:32 * j + 32, g % 2, :], q_now[:, j, :], kT_grp[:, g % 2, j, :],
                                                 start=True, stop=True, tile_position=(0, 32 * j))
                            last.then_inc(sc_mm, 1)

                        for i in range(RING):
                            turn(i)
                            if i % GRP == 0 and i:
                                group(i // GRP - 1)
                        group(RING // GRP - 1)
                    pe.wait_ge(new_taken, b)
                    for j in range(HP):
                        last = pe.matmul(ps_new[32 * j:32 * j + 32, 64:64 + T_S], q_now[:, j, :], m.kT[:, j, SEQ:T],
                                         start=True, stop=True, tile_position=(0, 32 * j))
                    last.then_inc(new_mm, 1)

                def v_pages(b, ahead):
                    pT_done = (pT_even, pT_odd)

                    def turn(g):
                        pe.wait_ge(pT_done[g % 2], b * (N_GRP // 2) + g // 2 + 1)
                        for k in range(GRP):
                            last = pe.transpose(ps_pT[:, g % 2, k * ROWS:(k + 1) * ROWS],
                                                probs[:, (g * GRP + k) * PAGE:(g * GRP + k + 1) * PAGE], m.ident[:, :])
                        last.then_inc(pT_mm, 1)

                    pe.wait_ge(exp_done, b + 1)
                    pe.wait_ge(new_taken, b + 2 if ahead else b + 1)
                    pe.wait_ge(oT_taken, b + 1)
                    turn(0)
                    pe.transpose(ps_new[0:T_S, 128:256], probs[:, PAST:PAST + T_S], m.ident[:, :]).then_inc(pTn_mm, 1)
                    for g in range(N_GRP):
                        if g + 1 < N_GRP:
                            turn(g + 1)
                        pe.wait_ge(pT_done[g % 2], b * (N_GRP // 2) + g // 2 + 2)
                        if g == 0:
                            pe.wait_ge(pTn_sb, b + 1)
                        for k in range(GRP):
                            n = g * GRP + k
                            pe.wait_ge(v_in[n % RING_V], 16 * (b * (NPG // RING_V) + n // RING_V + 1))
                            for j in range(HP):
                                at = k * ROWS + 32 * j
                                last = pe.matmul(ps_out[32 * j:32 * j + 32, 0:P], pT[:, g % 2, at:at + 32], v_places[n % RING_V][:, j * P:(j + 1) * P],
                                                 start=(n == 0), stop=False, skip_group_check=True, tile_position=(0, 32 * j))
                            last.then_inc(v_used, 1)
                    for j in range(HP):
                        last = pe.matmul(ps_out[32 * j:32 * j + 32, 0:P], pT_new[:, 32 * j:32 * j + 32], m.v[0:T_S, PT, j * P:(j + 1) * P],
                                         start=False, stop=True, skip_group_check=True, tile_position=(0, 32 * j))
                    last.then_inc(out_mm, 1)

                def out_transpose(b):
                    pe.wait_ge(o_rows_done, b + 1)
                    pe.transpose(ps_new[:, 256:256 + ROWS], o_rows[:, :], m.ident[:, :]).then_inc(oT_mm, 1)

                k_pages(0)
                with pe.Fori(0, DEC_B - 1) as b:
                    k_pages(b + 1)
                    v_pages(b, True)
                    out_transpose(b)
                v_pages(DEC_B - 1, False)
                out_transpose(DEC_B - 1)


BLK = 64
PAIR = P // BLK
MAX_BLK = PAIR * (T * TOPK // P + NE) + 2 * PAIR
TAB = 2 * P
assert MAX_BLK + 4 * PAIR <= TAB
RING_W = 4


def registers(nc, engine, table, at, n, low, high):
    return nc.values_load_multi_w_load_instructions(table[0:1, bass.ds(at, n)], engines=(engine,), min_val=low, max_val=high)[1]


def load_gate_up(sp, a, m, e, s):
    for i, name in enumerate(("w_gate_e", "w_up_e")):
        sp.dma_start(m.w_gu[:, s, i, :, :], a[name][0, bass.ds(e, 1)].rearrange("e (p k) n -> p (e k) n", k=KD)).then_inc(m.w_in[s], 16)


def load_down(sp, a, m, e, s):
    sp.dma_start(m.w_dn[:, s, :, :], a["w_down_e"][0, bass.ds(e, 1)].rearrange("e (p j) n -> p (e j) n", j=2)).then_inc(m.w_in[s], 16)


def mix_and_route(nc, a, o, m):
    sem = m.sem
    m.h_dram = nc.dram_tensor("h_dram", (T, D), F32, kind="Internal").ap()
    m.acc = nc.dram_tensor("acc_dram", (T + P, D), F32, kind="Internal").ap()
    psb = nc.alloc_sbuf_tensor
    m.pos = psb("pos", [P, TT, NE], F32)
    m.gate_parts = psb("gate_parts", [P, TT, NE, 3], mybir.dt.bfloat16)
    m.exp_tab = psb("exp_tab", [1, TAB], I32)
    m.use_tab = psb("use_tab", [1, TAB, 2], I32)
    m.load_tab = psb("load_tab", [1, NE + RING_W, 2], I32)
    m.loop_tab = psb("loop_tab", [1, 2], I32)
    m.w_gu = psb("w_gu", [P, RING_W, 2, KD, DE], F32)
    m.w_dn = psb("w_dn", [P, RING_W, 2, D], F32)
    m.w_in = [nc.alloc_semaphore(f"w_in_e{s}") for s in range(RING_W)]
    with ExitStack() as scope:
        sb = lambda *args: scope.enter_context(nc.sbuf_tensor(*args))
        w_out = m.w_gu[:, 0:2].rearrange("p s g k n -> p (s g k n)").rearrange("p (k n) -> p k n", k=8)
        w_gu_s = m.w_gu[:, 3].rearrange("p g k n -> p (g k n)").rearrange("p (k n) -> p k n", k=KD)
        w_dn_s = m.w_dn[:, 3]
        w_router = sb("w_router", [P, KD, NE], F32)
        ffn_row = m.w_dn[:, 2, 0, :]
        h_row, xn = m.w_dn[:, 0], m.w_dn[:, 1]
        zero = m.uT[:, 2:4, :].rearrange("p k n -> p (k n)")[:, 0:D]
        st = sb("st_f", [P, 3, TT], F32)
        score = sb("score", [P, TT, NE], F32)
        biased = sb("biased", [P, TT, NE], F32)
        top = sb("top", [P, TT, 8], F32)
        mask = sb("mask", [P, TT, NE], F32)
        gate = sb("gate", [P, TT, NE], F32)
        rest = sb("rest", [P, TT, NE], F32)
        part = sb("part", [P, TT, NE], F32)
        gsum = sb("gsum", [P, 2, TT], F32)
        cnt = sb("cnt", [P, 11, NE], F32)
        blk_no = sb("blk_no", [P, 2], F32)
        exp_row = sb("exp_row", [P, NE], F32)
        n_i = sb("n_i", [P, 4], I32)
        n_f = sb("n_f", [P, 3], F32)
        hits = sb("hits", [P, 5, NE], F32)
        found = sb("found", [P, 6, NE], F32)
        entry = sb("entry", [P, 6], F32)
        entry_bc = sb("entry_bc", [P, 6, P], F32)
        tab_i = sb("tab_i", [1, 6, P], I32)
        free_i = sb("free_i", [1, NE + 2], I32)
        ps = scope.enter_context(nc.psum_tensor("ps_e8", [P, 8, 512], F32))
        sq = (m.kT, m.qT)
        hT = m.mixT
        actT = m.uT
        inv = m.v[:, :, :].rearrange("p t n -> p (t n)")[:, 0:2 * T].rearrange("p (a n) -> p a n", a=2)

        w_in_e, ws_in, misc_in = sem("w_out_in"), sem("ws_in"), sem("misc_in")
        sq_done, ms_mm, ms_done, root_done, mix_done = (sem(x) for x in ("sqe", "ms_mm", "mse", "roote", "mix_done"))
        o_mm, x1_done, ss_done, ms2, root2, xn2, tr_mm, hT_done, h_done = (
            sem(x) for x in ("oe_mm", "x1_done", "ss_e", "ms2", "root2", "xn2", "tr_e", "hT_done", "h_done"))
        h_out = [sem("h_out0"), sem("h_out1")]
        r_mm, score_done, mask_done, rank_mm, cum_done, exp_mm = (
            sem(x) for x in ("r_mm", "score_done", "mask_done", "rank_mm", "cum_done", "exp_mm"))
        gu_mm, silu_done, act_done, dn_mm, acc_done, acc_out, zero_done = (
            sem(x) for x in ("gus_mm", "silu_s", "act_s", "dns_mm", "acc_done", "acc_out", "zero_done"))
        iota_done, tables_done = sem("iota_done"), sem("tables_done")

        with nc.Block(no_gpsimd_drain=True) as block:

            @block.sync
            def _(sp):
                sp.dma_start(w_out[:, :, :], a["w_out"][0].rearrange("(k p) n -> p k n", p=P)).then_inc(w_in_e, 16)
                sp.dma_start(w_router[:, :, :], a["w_router"][0].rearrange("(k p) n -> p k n", p=P)).then_inc(misc_in, 16)
                sp.dma_start(w_gu_s[:, :, 0:DE], a["w_gate_s"][0].rearrange("(k p) n -> p k n", p=P)).then_inc(ws_in, 16)
                sp.dma_start(w_gu_s[:, :, DE:2 * DE], a["w_up_s"][0].rearrange("(k p) n -> p k n", p=P)).then_inc(ws_in, 16)
                sp.dma_start(w_dn_s[:, :, :], a["w_down_s"][0].rearrange("(k p) n -> p k n", p=P)).then_inc(ws_in, 16)
                sp.dma_start(ffn_row[:, :], a["norm_ffn_w"][0].partition_broadcast(P)).then_inc(misc_in, 16)
                sp.wait_ge(zero_done, 1)
                sp.dma_start(m.acc[T:T + P, :], zero[:, :]).then_inc(acc_out, 16)
                for t in range(TT):
                    sp.wait_ge(h_done, t + 1)
                    sp.dma_start(m.h_dram[t * P:t * P + rows(t), :], h_row[0:rows(t), t % 2, :]).then_inc(h_out[t % 2], 16)
                sp.wait_ge(o_mm, TT)
                sp.wait_ge(tr_mm, 2 * TT)
                sp.wait_ge(h_out[0], 16 * 3)
                sp.wait_ge(h_out[1], 16 * 2)
                sp.wait_ge(tables_done, 1)
                for s in range(PAIR):
                    expert, _ = registers(nc, mybir.EngineType.SP, m.load_tab[:, :, :].rearrange("o b c -> o (b c)"), 2 * s, 2, 0, TAB)
                    expert = nc.s_assert_within(expert, 0, NE - 1)
                    load_gate_up(sp, a, m, expert, s)
                    load_down(sp, a, m, expert, s)
                for t in range(TT):
                    sp.wait_ge(acc_done, t + 1)
                    sp.dma_start(m.acc[t * P:t * P + rows(t), :], m.xres[0:rows(t), t, :]).then_inc(acc_out, 16)
                sp.wait_ge(acc_out, 16 * (TT + 1))

            @block.gpsimd
            def _(pool):
                pool.memset(zero[:, :], 0.0).then_inc(zero_done, 1)
                pool.memset(mask[:, :, :], 0.0)
                pool.memset(gate[:, :, :], 0.0)
                pool.iota(blk_no[:, :], [[P, 2]], base=0, channel_multiplier=1, allow_small_or_imprecise_dtypes=True)
                pool.iota(exp_row[:, :], [[1, NE]], base=0, channel_multiplier=0, allow_small_or_imprecise_dtypes=True)
                pool.drain()
                pool.sem_inc(iota_done, 1)

            @block.scalar
            def _(act):
                for i in range(2):
                    act.activation(sq[i][:, :, :], m.mixT[:, 4 * i:4 * i + 4, :], ACT.Square).then_inc(sq_done, 1)
                act.wait_ge(ms_done, 1)
                act.activation(inv, inv, ACT.Sqrt).then_inc(root_done, 1)
                for t in range(TT):
                    n = rows(t)
                    act.wait_ge(x1_done, t + 1)
                    act.activation(h_row[0:n, t % 2, :], m.xres[0:n, t, :], ACT.Square, accum_out=st[0:n, 0, t:t + 1]).then_inc(ss_done, 1)
                    act.wait_ge(ms2, t + 1)
                    act.activation(st[0:n, 2, t:t + 1], st[0:n, 1, t:t + 1], ACT.Sqrt).then_inc(root2, 1)
                    if t + 1 < TT:
                        act.wait_ge(h_done, t)
                        if t >= 1:
                            act.wait_ge(h_out[(t + 1) % 2], 16 * ((t + 1) // 2))
                for t in range(TT):
                    n = rows(t)
                    if t == 0:
                        act.wait_ge(r_mm, TT)
                    act.activation(score[0:n, t, :], ps[0:n, 7, t * NE:(t + 1) * NE], ACT.Sigmoid).then_inc(score_done, 1)
                for f in range(2):
                    act.wait_ge(gu_mm, f + 1)
                    b = 4 * f
                    act.activation(actT[:, f, 0:SEQ], ps[:, b, :], ACT.Silu)
                    act.activation(actT[:, f, SEQ:T], ps[:, b + 1, 0:T_S], ACT.Silu).then_inc(silu_done, 1)

            @block.vector
            def _(dve):
                tt = dve.tensor_tensor
                dve.wait_ge(ms_mm, 1)
                for i in range(2):
                    dve.tensor_scalar(inv[:, i, 0:SEQ], ps[:, i, :], 1.0 / DA, EPS, ALU.mult, ALU.add)
                    last = dve.tensor_scalar(inv[:, i, SEQ:T], ps[:, 2, i * T_S:(i + 1) * T_S], 1.0 / DA, EPS, ALU.mult, ALU.add)
                last.then_inc(ms_done, 1)
                dve.wait_ge(root_done, 1)
                dve.reciprocal(inv, inv)
                dve.drain()
                for k in range(8):
                    c = m.col["mix_out"] + k
                    dve.scalar_tensor_tensor(m.mixT[:, k, :], m.mixT[:, k, :], m.columns[:, c:c + 1], inv[:, k // 4, :],
                                             ALU.mult, ALU.mult).then_inc(mix_done, 1)
                dve.wait_ge(misc_in, 32)
                for t in range(TT):
                    n = rows(t)
                    dve.wait_ge(o_mm, t + 1)
                    tt(m.xres[0:n, t, :], m.xres[0:n, t, :], ps[0:n, 3 + 2 * (t % 2):5 + 2 * (t % 2), :].rearrange("p a n -> p (a n)"), ALU.add).then_inc(x1_done, 1)
                    dve.wait_ge(ss_done, t + 1)
                    dve.tensor_scalar(st[0:n, 1, t:t + 1], st[0:n, 0, t:t + 1], 1.0 / D, EPS, ALU.mult, ALU.add).then_inc(ms2, 1)
                    dve.wait_ge(root2, t + 1)
                    dve.reciprocal(st[0:n, 0, t:t + 1], st[0:n, 2, t:t + 1])
                    if t >= 2:
                        dve.wait_ge(tr_mm, 2 * (t - 1))
                    dve.drain()
                    dve.tensor_scalar(xn[0:n, t % 2, :], m.xres[0:n, t, :], st[0:n, 0, t:t + 1], None, ALU.mult).then_inc(xn2, 1)
                    dve.drain()
                    tt(h_row[0:n, t % 2, :], xn[0:n, t % 2, :], ffn_row[0:n, :], ALU.mult).then_inc(h_done, 1)
                    for half in range(2):
                        dve.wait_ge(tr_mm, 2 * t + half + 1)
                        c = m.col["norm_ffn"] + 4 * half
                        w = m.columns[:, c:c + 4].unsqueeze(2).to_broadcast((P, 4, n))
                        tt(hT[:, 4 * half:4 * half + 4, cols(t)], ps[:, half, :].rearrange("p (k n) -> p k n", n=P)[:, :, 0:n], w, ALU.mult).then_inc(hT_done, 1)
                dve.wait_ge(iota_done, 1)
                for t in range(TT):
                    n = rows(t)
                    s, b, v = score[0:n, t, :], biased[0:n, t, :], top[0:n, t, :]
                    dve.wait_ge(score_done, t + 1)
                    tt(b, s, m.router_bias[0:n, :], ALU.add)
                    dve.drain()
                    dve.max(v, b)
                    dve.drain()
                    dve.match_replace(rest[0:n, t, :], v, b, MASKED)
                    dve.drain()
                    tt(mask[0:n, t, :], rest[0:n, t, :], b, ALU.is_lt)
                    dve.drain()
                    tt(gate[0:n, t, :], s, mask[0:n, t, :], ALU.mult).then_inc(mask_done, 1)
                    dve.drain()
                    dve.tensor_reduce(gsum[0:n, 0, t:t + 1], gate[0:n, t, :], AX.X, ALU.add)
                    dve.drain()
                    dve.reciprocal(gsum[0:n, 1, t:t + 1], gsum[0:n, 0, t:t + 1])
                    dve.tensor_scalar(gate[0:n, t, :], gate[0:n, t, :], 2.5, None, ALU.mult)
                    dve.drain()
                    dve.tensor_scalar(gate[0:n, t, :], gate[0:n, t, :], gsum[0:n, 1, t:t + 1], None, ALU.mult)
                dve.drain()
                dve.tensor_copy(m.gate_parts[:, :, :, 0], gate[:, :, :])
                dve.drain()
                tt(rest[:, :, :], gate[:, :, :], m.gate_parts[:, :, :, 0], ALU.subtract)
                dve.drain()
                dve.tensor_copy(m.gate_parts[:, :, :, 1], rest[:, :, :])
                dve.drain()
                tt(part[:, :, :], rest[:, :, :], m.gate_parts[:, :, :, 1], ALU.subtract)
                dve.drain()
                dve.tensor_copy(m.gate_parts[:, :, :, 2], part[:, :, :])
                for f in range(2):
                    dve.wait_ge(silu_done, f + 1)
                    tt(actT[:, f, 0:SEQ], actT[:, f, 0:SEQ], ps[:, 4 * f + 2, :], ALU.mult)
                    tt(actT[:, f, SEQ:T], actT[:, f, SEQ:T], ps[:, 4 * f + 1, 64:64 + T_S], ALU.mult).then_inc(act_done, 1)
                count, n_big, tmp, small, small_no, paired, paired_no, blocks, end, first, order = (cnt[:, i, :] for i in range(11))
                dve.wait_ge(rank_mm, 1)
                dve.tensor_copy(count, ps[:, 3, TT * NE:(TT + 1) * NE])
                dve.memset(n_big, 1.0)
                dve.drain()
                for k in range(1, -(-T // P)):
                    dve.tensor_scalar(tmp, count, float(k * P), None, ALU.is_gt)
                    dve.drain()
                    tt(n_big, n_big, tmp, ALU.add)
                    dve.drain()
                dve.tensor_scalar(small, count, float(BLK), None, ALU.is_le)
                dve.drain()
                dve.tensor_tensor_scan(small_no, m.ones[:, 0:NE], small, 0.0, ALU.mult, ALU.add)
                dve.drain()
                dve.tensor_copy(n_i[:, 0:1], small_no[:, NE - 1:NE])
                dve.drain()
                dve.tensor_scalar(n_i[:, 1:2], n_i[:, 0:1], 2 * P - 2 * PAIR, None, ALU.bitwise_and)
                dve.drain()
                dve.tensor_copy(n_f[:, 0:1], n_i[:, 1:2])
                dve.drain()
                dve.tensor_scalar(n_f[:, 1:2], n_f[:, 0:1], float(2 * PAIR), None, ALU.max)
                dve.tensor_scalar(paired, small_no, n_f[:, 0:1], None, ALU.is_le)
                dve.drain()
                tt(paired, paired, small, ALU.mult)
                dve.drain()
                dve.tensor_tensor_scan(paired_no, m.ones[:, 0:NE], paired, 0.0, ALU.mult, ALU.add)
                dve.tensor_scalar(tmp, paired, -float(PAIR), float(PAIR), ALU.mult, ALU.add)
                dve.drain()
                tt(blocks, n_big, tmp, ALU.mult)
                tt(order, exp_row[:, :], paired_no, ALU.subtract)
                dve.drain()
                dve.tensor_tensor_scan(end, m.ones[:, 0:NE], blocks, 0.0, ALU.mult, ALU.add)
                dve.tensor_scalar(order, order, n_f[:, 0:1], None, ALU.add)
                dve.drain()
                dve.tensor_scalar(end, end, n_f[:, 1:2], None, ALU.add)
                dve.drain()
                dve.tensor_copy(n_f[:, 2:3], end[:, NE - 1:NE])
                tt(first, end, blocks, ALU.subtract)
                dve.drain()
                for row in (order, first):
                    tt(tmp, small_no, row, ALU.subtract)
                    dve.drain()
                    dve.tensor_scalar(tmp, tmp, 1.0, None, ALU.subtract)
                    dve.drain()
                    tt(tmp, tmp, paired, ALU.mult)
                    dve.drain()
                    tt(row, row, tmp, ALU.add)
                    dve.drain()
                tt(end, first, blocks, ALU.add)
                dve.drain()
                tt(end, end, paired, ALU.add)
                dve.tensor_scalar(tmp, first, float(BLK), 1.0, ALU.mult, ALU.add)
                dve.drain()
                for t in range(TT):
                    tt(m.pos[:, t, :], ps[:, 3, t * NE:(t + 1) * NE], tmp, ALU.add)
                dve.drain()
                tt(m.pos[:, :, :], m.pos[:, :, :], mask[:, :, :], ALU.mult)
                dve.drain()
                dve.tensor_scalar(m.pos[:, :, :], m.pos[:, :, :], 1.0, None, ALU.subtract)
                for i in range(2):
                    dve.tensor_scalar(hits[:, i, :], first, blk_no[:, i:i + 1], None, ALU.is_le)
                    dve.tensor_scalar(hits[:, 3 + i, :], end, blk_no[:, i:i + 1], None, ALU.is_gt)
                dve.tensor_scalar(hits[:, 2, :], order, blk_no[:, 0:1], None, ALU.is_equal)
                dve.drain()
                tt(hits[:, 0:2, :], hits[:, 0:2, :], hits[:, 3:5, :], ALU.mult)
                dve.drain()
                for i, row in ((0, exp_row[:, :]), (3, order)):
                    tt(found[:, i:i + 3, :], hits[:, 0:3, :], row.unsqueeze(1).to_broadcast((P, 3, NE)), ALU.mult)
                dve.drain()
                tt(found[:, 5, :], hits[:, 2, :], end, ALU.mult)
                dve.drain()
                dve.tensor_reduce(entry[:, :], found[:, :, :], AX.X, ALU.add)
                dve.drain()
                for i in range(6):
                    last = dve.tensor_scalar(entry_bc[:, i, :], m.ones[:, :], entry[:, i:i + 1], None, ALU.mult)
                last.then_inc(cum_done, 1)
                dve.wait_ge(exp_mm, 1)
                dve.tensor_copy(tab_i[:, 0:4, :].rearrange("o a n -> o (a n)"), ps[0:1, 5, :])
                dve.tensor_copy(tab_i[:, 4:6, :].rearrange("o a n -> o (a n)"), ps[0:1, 6, 0:2 * P])
                dve.tensor_copy(n_i[:, 2:4], n_f[:, 1:3])
                dve.memset(m.load_tab[:, :, :], 1)
                dve.drain()
                dve.tensor_copy(m.exp_tab[:, :], tab_i[:, 0:2, :].rearrange("o a n -> o (a n)"))
                dve.tensor_copy(m.load_tab[:, 0:NE, 0], tab_i[:, 2, 0:NE])
                use = tab_i[:, 3:5, :].rearrange("o a n -> o (a n)")
                dve.tensor_scalar(m.use_tab[:, :, 0], use, 1.0, None, ALU.add)
                dve.tensor_scalar(m.use_tab[:, :, 1], use, RING_W - 1, None, ALU.bitwise_and)
                dve.tensor_scalar(free_i[:, 0:NE], tab_i[:, 5, 0:NE], float(PAIR - 1), None, ALU.add)
                dve.tensor_scalar(free_i[:, NE:NE + 2], n_i[0:1, 2:4], float(2 * PAIR - 1), None, ALU.add)
                dve.drain()
                dve.tensor_scalar(m.load_tab[:, RING_W:RING_W + NE, 1], free_i[:, 0:NE], 1, None, ALU.arith_shift_right)
                dve.tensor_scalar(m.loop_tab[:, :], free_i[:, NE:NE + 2], 2, None, ALU.arith_shift_right)
                dve.drain()
                dve.sem_inc(tables_done, 1)
                for t in range(TT):
                    n = rows(t)
                    dve.wait_ge(dn_mm, t + 1)
                    tt(m.xres[0:n, t, :], m.xres[0:n, t, :], ps[0:n, 2 * (t % 2):2 * (t % 2) + 2, :].rearrange("p a n -> p (a n)"), ALU.add).then_inc(acc_done, 1)

            @block.tensor
            def _(pe):
                for i in range(2):
                    pe.wait_ge(sq_done, i + 1)
                    for k in range(4):
                        pe.matmul(ps[:, i, :], m.ones[:, :], sq[i][:, k, 0:SEQ], start=(k == 0), stop=(k == 3))
                    for k in range(4):
                        last = pe.matmul(ps[:, 2, i * T_S:(i + 1) * T_S], m.ones[:, :], sq[i][:, k, SEQ:T], start=(k == 0), stop=(k == 3))
                last.then_inc(ms_mm, 1)
                pe.wait_ge(w_in_e, 16)
                pe.wait_ge(ms_done, 1)

                def transposes(t):
                    n = rows(t)
                    pe.wait_ge(xn2, t + 1)
                    for half in range(2):
                        if t >= 1:
                            pe.wait_ge(hT_done, 2 * (t - 1) + half + 1)
                        for j in range(4):
                            k = 4 * half + j
                            last = pe.transpose(ps[:, half, j * P:j * P + n], xn[0:n, t % 2, k * P:(k + 1) * P], m.ident[0:n, 0:n])
                        last.then_inc(tr_mm, 1)

                pe.wait_ge(mix_done, 8)
                for t in range(TT):
                    n = rows(t)
                    if t >= 2:
                        pe.wait_ge(x1_done, t - 1)
                    for half in range(2):
                        for k in range(8):
                            last = pe.matmul(ps[0:n, 3 + 2 * (t % 2) + half, :], m.mixT[:, k, cols(t)], w_out[:, k, half * 512:(half + 1) * 512],
                                             start=(k == 0), stop=(k == 7))
                    last.then_inc(o_mm, 1)
                    if t >= 1:
                        transposes(t - 1)
                transposes(TT - 1)
                pe.wait_ge(misc_in, 32)
                pe.wait_ge(hT_done, 2 * TT)
                for t in range(TT):
                    n = rows(t)
                    for k in range(KD):
                        last = pe.matmul(ps[0:n, 7, t * NE:(t + 1) * NE], hT[:, k, cols(t)], w_router[:, k, :], start=(k == 0), stop=(k == KD - 1))
                    last.then_inc(r_mm, 1)
                pe.wait_ge(ws_in, 48)
                for f in range(2):
                    for i, bank in ((0, 4 * f), (1, 4 * f + 2)):
                        for k in range(KD):
                            w = w_gu_s[:, k, i * DE + f * P:i * DE + (f + 1) * P]
                            pe.matmul(ps[:, bank, :], w, hT[:, k, 0:SEQ], start=(k == 0), stop=(k == KD - 1))
                        for k in range(KD):
                            w = w_gu_s[:, k, i * DE + f * P:i * DE + (f + 1) * P]
                            last = pe.matmul(ps[:, 4 * f + 1, i * 64:i * 64 + T_S], w, hT[:, k, SEQ:T], start=(k == 0), stop=(k == KD - 1))
                    last.then_inc(gu_mm, 1)
                pe.wait_ge(mask_done, TT)
                for t in range(TT + 1):
                    tiles = range(min(t + 1, TT))
                    for s in tiles:
                        last = pe.matmul(ps[:, 3, t * NE:(t + 1) * NE], (m.tri_strict if s == t else m.ones)[:, :], mask[:, s, :],
                                         start=(s == 0), stop=(s == tiles[-1]))
                last.then_inc(rank_mm, 1)
                pe.wait_ge(cum_done, 1)
                pe.wait_ge(act_done, 2)
                for i in range(6):
                    last = pe.matmul(ps[:, 5 + i // 4, (i % 4) * P:(i % 4 + 1) * P], entry_bc[:, i, :], m.ident[:, :], start=True, stop=True)
                last.then_inc(exp_mm, 1)
                for t in range(TT):
                    n = rows(t)
                    if t >= 2:
                        pe.wait_ge(acc_done, t - 1)
                    for half in range(2):
                        for j in range(2):
                            last = pe.matmul(ps[0:n, 2 * (t % 2) + half, :], actT[:, j, cols(t)], w_dn_s[:, j, half * 512:(half + 1) * 512],
                                             start=(j == 0), stop=(j == 1))
                    last.then_inc(dn_mm, 1)


def experts(nc, a, o, m):
    sem = m.sem
    BF = mybir.dt.bfloat16
    ENG = mybir.EngineType
    use_tab = m.use_tab[:, :, :].rearrange("o b c -> o (b c)")
    load_tab = m.load_tab[:, :, :].rearrange("o b c -> o (b c)")
    n_rounds = NE // RING_W
    with ExitStack() as scope:
        sb = lambda *args: scope.enter_context(nc.sbuf_tensor(*args))
        w_gu, w_dn, w_in = m.w_gu, m.w_dn, m.w_in
        xg, ys = m.xres[:, 0:2, :], m.xres[:, 2:4, :]
        xgT = m.mixT[:, :, :].rearrange("p k n -> p (k n)")[:, 0:2 * KD * P].rearrange("p (b k n) -> p b k n", b=2, k=KD)
        sil = sb("sil", [P, DE], F32)
        act_in = sb("act_in", [P, DE], F32)
        aT = sb("aT_e", [P, 2, P], F32)
        slots = sb("slots", [P, BLK], F32)
        base = sb("base", [P, PAIR], F32)
        posn = sb("posn", [P, PAIR, TT], F32)
        sel = sb("sel", [P, TT, P], BF)
        tg = sb("tg", [P, TT, 9], BF)
        tok_f = sb("tok_f", [P, TT], F32)
        tok_i = sb("tok_i", [P, 3, TT], I32)
        info = sb("info", [P, 2, 12], F32)
        gate = sb("gate_e", [P, 1], F32)
        idx = sb("idx", [P, 2, 1], I32)
        spare = sb("spare", [BLK, PAIR], F32)
        empty = sb("empty", [BLK, PAIR], F32)
        row_f = sb("row_f", [BLK, 2, PAIR], F32)
        sidx = sb("sidx", [BLK, PAIR, 2], I32)
        ps_gu, ps_aT, ps_idx = (scope.enter_context(nc.psum_tensor(x, [P, 512], F32)) for x in ("ps_gu", "ps_aT", "ps_idx"))
        ps_xT = scope.enter_context(nc.psum_tensor("ps_xT", [P, 2, 512], F32))
        ps_y = scope.enter_context(nc.psum_tensor("ps_y", [P, 2, 512], F32))

        w_ready = sem("w_ready")
        const_done, sel_done, idx_mm, idx_done = sem("const_e"), sem("sel_done"), sem("idx_mm"), sem("idx_done")
        gathered = [sem("gathered0"), sem("gathered1")]
        tr_mm, xT_act, xT_dve = sem("tr_mm_e"), sem("xT_act"), sem("xT_dve")
        gu_mm, silu_done, a_done, aT_mm, aT_done = (sem(x) for x in ("gu_mm", "silu_e", "a_done", "aT_mm", "aT_done"))
        dn_mm, y_act, y_dve, row_done = (sem(x) for x in ("dn_mm_e", "y_act", "y_dve", "row_done"))
        added = [sem("added_a"), sem("added_b")]
        scattered = sem("scattered")
        pool_turns = sem("pool_turns")

        def loops(eng):
            return registers(nc, eng, m.loop_tab, 0, 2, 1, TAB // (2 * PAIR) - 2)

        with nc.Block(no_gpsimd_drain=True) as block:

            @block.sync
            def _(sp):
                sp.wait_ge(idx_done, 2)
                for s in range(PAIR, RING_W):
                    expert, _ = registers(nc, ENG.SP, load_tab, 2 * s, 2, 0, TAB)
                    expert = nc.s_assert_within(expert, 0, NE - 1)
                    load_gate_up(sp, a, m, expert, s)
                    load_down(sp, a, m, expert, s)
                for s in range(RING_W - 1):
                    sp.wait_ge(w_in[s], 48)
                    sp.sem_inc(w_ready, 1)
                with sp.Fori(1, n_rounds) as r:
                    for s in range(RING_W):
                        expert, used = registers(nc, ENG.SP, load_tab, r * (2 * RING_W) + 2 * s, 2, 0, TAB)
                        expert = nc.s_assert_within(expert, 0, NE - 1)
                        used = nc.s_assert_within(used, 1, TAB)
                        sp.wait_ge(gu_mm, used)
                        load_gate_up(sp, a, m, expert, s)
                        sp.wait_ge(w_in[s - 1], 48 * (r + 1) if s else 48 * r)
                        sp.sem_inc(w_ready, 1)
                        sp.wait_ge(dn_mm, used * 2)
                        load_down(sp, a, m, expert, s)
                sp.wait_ge(w_in[RING_W - 1], 48 * n_rounds)
                sp.sem_inc(w_ready, 1)
                _, n_loops = loops(ENG.SP)
                all_gathers, all_adds = sp.to_reg(n_loops * 16 + 16), sp.to_reg(n_loops * 32)
                for u in range(2):
                    sp.wait_ge(gathered[u], all_gathers)
                for h in range(PAIR):
                    sp.wait_ge(added[h], all_adds)
                sp.dma_start(o["y_prompt"][0], m.acc[0:SEQ, :]).then_inc(w_in[0], 16)
                sp.dma_start(o["y_sample"].rearrange("b s d -> (b s) d"), m.acc[SEQ:T, :]).then_inc(w_in[0], 16)
                sp.wait_ge(w_in[0], 48 * n_rounds + 32)

            @block.gpsimd
            def _(pool):
                pool.sem_inc(scattered, 2)
                _, n_loops = loops(ENG.Pool)
                pool.iota(slots[:, :], [[1, BLK]], base=0, channel_multiplier=0, allow_small_or_imprecise_dtypes=True)
                pool.iota(spare[:, :], [[BLK, PAIR]], base=T, channel_multiplier=1, allow_small_or_imprecise_dtypes=True)
                pool.iota(tok_i[:, 0, :], [[P, TT]], base=0, channel_multiplier=1)
                pool.iota(base[:, :], [[BLK, PAIR]], base=0, channel_multiplier=0, allow_small_or_imprecise_dtypes=True)
                pool.memset(tg[:, :, 2:3], 1.0)
                pool.drain()
                pool.sem_inc(const_done, 1)

                def gather(b, n_idx):
                    pool.wait_ge(idx_done, n_idx)
                    pool.sem_inc(pool_turns, 1)
                    pool.indirect_dma_start(xg[:, b, :], None, m.h_dram, bass.IndirectOffsetOnAxis(ap=idx[:, b, :], axis=0),
                                            bounds_check=last_token).then_inc(gathered[b], 16)

                last_token, last_row = pool.to_reg(T - 1), pool.to_reg(T + P - 1)
                for u in range(2):
                    gather(u, u + 1)
                with pool.Fori(0, n_loops) as i:
                    for u in range(2):
                        gather(u, i * 2 + (u + 3))
                        pool.wait_ge(y_act, i * 2 + (u + 1) + 1)
                        pool.wait_ge(y_dve, i * 2 + (u + 1) + 1)
                        pool.wait_ge(row_done, i * 2 + (u + 1))
                        for h in range(PAIR):
                            pool.sem_inc(pool_turns, 1)
                            pool.indirect_dma_start(m.acc, bass.IndirectOffsetOnAxis(ap=sidx[:, h, u:u + 1], axis=0),
                                                    ys[h * BLK:(h + 1) * BLK, u, :], None, bounds_check=last_row,
                                                    compute_op=ALU.add).then_inc(added[h], 16)
                            pool.wait_ge(added[h], i * 32 + 16 * (u + 1))
                        pool.sem_inc(scattered, 1)

            @block.scalar
            def _(act):
                act.sem_inc(y_act, 1)
                def xT(b, tr):
                    act.wait_ge(tr_mm, tr)
                    act.copy(xgT[:, b, 0:4, :].rearrange("p k n -> p (k n)"), ps_xT[:, 0, :]).then_inc(xT_act, 1)

                _, n_loops = loops(ENG.Activation)
                xT(0, 1)
                with act.Fori(0, n_loops) as i:
                    for u in range(2):
                        act.wait_ge(gu_mm, i * 2 + (u + 1))
                        act.activation(sil[:, :], ps_gu[:, 0:DE], ACT.Silu).then_inc(silu_done, 1)
                        xT(1 - u, i * 4 + (2 * u + 3))
                        act.wait_ge(dn_mm, i * 4 + (2 * u + 1))
                        act.wait_ge(scattered, i * 2 + (u + 1))
                        act.wait_ge(row_done, i * 2 + (u + 1))
                        act.activation(ys[:, u, 0:512], ps_y[:, 0, :], ACT.Copy, scale=gate[:, 0:1]).then_inc(y_act, 1)

            @block.vector
            def _(dve):
                dve.sem_inc(y_dve, 1)
                _, n_loops = loops(ENG.DVE)
                dve.wait_ge(const_done, 1)
                dve.tensor_scalar(tok_i[:, 1, :], tok_i[:, 0, :], 3, None, ALU.arith_shift_right)
                dve.tensor_scalar(tok_i[:, 2, :], tok_i[:, 0, :], 7, None, ALU.bitwise_and)
                dve.drain()
                dve.tensor_copy(tg[:, :, 0], tok_i[:, 1, :])
                dve.tensor_copy(tg[:, :, 1], tok_i[:, 2, :])
                dve.drain()

                def select(n):
                    experts_of = registers(nc, ENG.DVE, m.exp_tab, n * PAIR, PAIR, 0, NE - 1)
                    if not isinstance(n, int) or n:
                        dve.wait_ge(idx_mm, n)
                    for h in range(PAIR):
                        at = bass.ds(experts_of[h], 1)
                        dve.tensor_scalar(posn[:, h, :], m.pos[:, :, at].rearrange("p t e -> p (t e)"), base[:, h:h + 1], None, ALU.subtract)
                        dve.tensor_copy(tg[:, :, 3 + 3 * h:6 + 3 * h], m.gate_parts[:, :, at, :].rearrange("p t e c -> p (t e) c"))
                    dve.drain()
                    for h in range(PAIR):
                        last = dve.tensor_tensor(sel[:, :, h * BLK:(h + 1) * BLK], slots[:, :].unsqueeze(1).to_broadcast((P, TT, BLK)),
                                                 posn[:, h, :].unsqueeze(2).to_broadcast((P, TT, BLK)), ALU.is_equal)
                    last.then_inc(sel_done, 1)
                    dve.tensor_scalar(base[:, :], base[:, :], float(P), None, ALU.add)

                def indices(b, n):
                    dve.wait_ge(idx_mm, n)
                    dve.tensor_copy(info[:, b, 0:9], ps_idx[:, 0:9])
                    dve.tensor_copy(info[0:BLK, b, 9:12], ps_idx[0:BLK, 16:19])
                    dve.drain()
                    dve.scalar_tensor_tensor(idx[:, b, :], info[:, b, 0:1], 8.0, info[:, b, 1:2], ALU.mult, ALU.add).then_inc(idx_done, 1)

                def xT(b, tr):
                    dve.wait_ge(tr_mm, tr)
                    dve.tensor_copy(xgT[:, b, 4:8, :].rearrange("p k n -> p (k n)"), ps_xT[:, 1, :]).then_inc(xT_dve, 1)

                for u in range(2):
                    select(u)
                    indices(u, u + 1)
                xT(0, 2)
                with dve.Fori(0, n_loops) as i:
                    for u in range(2):
                        step = i * 2 + u
                        select(step + 2)
                        dve.wait_ge(y_act, step + 1)
                        for h in range(PAIR):
                            hi, lo, there = (info[0:BLK, u, 9 * h + c:9 * h + c + 1] for c in range(3))
                            dve.tensor_scalar(empty[:, h:h + 1], there, -1.0, 1.0, ALU.mult, ALU.add)
                            dve.scalar_tensor_tensor(row_f[:, 0, h:h + 1], hi, 8.0, lo, ALU.mult, ALU.add)
                            dve.tensor_reduce(gate[h * BLK:(h + 1) * BLK, :], info[h * BLK:(h + 1) * BLK, u, 3 + 3 * h:6 + 3 * h], AX.X, ALU.add)
                        dve.drain()
                        dve.wait_ge(scattered, step + 1)
                        dve.tensor_tensor(row_f[:, 1, :], empty[:, :], spare[:, :], ALU.mult)
                        dve.drain()
                        dve.tensor_tensor(sidx[:, :, u], row_f[:, 0, :], row_f[:, 1, :], ALU.add).then_inc(row_done, 1)
                        dve.wait_ge(silu_done, step + 1)
                        dve.tensor_tensor(act_in[:, :], sil[:, :], ps_gu[:, DE:2 * DE], ALU.mult).then_inc(a_done, 1)
                        dve.wait_ge(aT_mm, step + 1)
                        dve.tensor_copy(aT[:, :, :].rearrange("p j n -> p (j n)"), ps_aT[:, 0:2 * P]).then_inc(aT_done, 1)
                        xT(1 - u, i * 4 + (2 * u + 4))
                        dve.wait_ge(dn_mm, i * 4 + (2 * u + 2))
                        dve.tensor_scalar(ys[:, u, 512:D], ps_y[:, 1, :], gate[:, 0:1], None, ALU.mult).then_inc(y_dve, 1)
                        indices(u, step + 3)

            @block.tensor
            def _(pe):
                n_paired, n_loops = loops(ENG.PE)

                def find(n):
                    pe.wait_ge(sel_done, n + 1)
                    if not isinstance(n, int) or n:
                        pe.wait_ge(idx_done, n)
                    for out, at in ((ps_idx[:, 0:9], slice(0, P)), (ps_idx[0:BLK, 16:19], slice(BLK, P))):
                        for t in range(TT):
                            last = pe.matmul(out, sel[0:rows(t), t, at], tg[0:rows(t), t, 0:9 if at.start == 0 else 3], start=(t == 0), stop=(t == TT - 1))
                    last.then_inc(idx_mm, 1)

                def transposes(b, got, taken, halves=(0, 1)):
                    pe.wait_ge(gathered[b], got)
                    for half in halves:
                        if taken is not None:
                            pe.wait_ge((xT_act, xT_dve)[half], taken)
                        for c in range(4):
                            last = pe.transpose(ps_xT[:, half, c * P:(c + 1) * P], xg[:, b, 4 * half + c:D:KD], m.ident[:, :])
                        last.then_inc(tr_mm, 1)

                find(0)
                find(1)
                transposes(0, 16, None)

                def step_of(i, u, paired):
                    step = i * 2 + u
                    if paired:
                        places = [slice(PAIR * u + h, PAIR * u + h + 1) for h in range(PAIR)]
                        halves = [(slice(h * BLK, (h + 1) * BLK), places[h], (0, h * BLK)) for h in range(PAIR)]
                        needed = i * (2 * PAIR) + PAIR * (u + 1)
                    else:
                        needed, place = registers(nc, ENG.PE, use_tab, step * (2 * PAIR), 2, 0, NE)
                        needed = nc.s_assert_within(needed, 1, NE)
                        halves = [(slice(0, P), bass.ds(nc.s_assert_within(place, 0, RING_W - 1), 1), None)]
                    pe.wait_ge(w_ready, needed)
                    pe.wait_ge(xT_act, step + 1)
                    pe.wait_ge(xT_dve, step + 1)
                    for k in range(KD):
                        for at, place, tile in halves:
                            last = pe.matmul(ps_gu[at, :].rearrange("p (g n) -> p g n", g=2), xgT[:, u, k, at],
                                             w_gu[:, place, :, k, :].rearrange("p s g n -> p (s g) n"),
                                             start=(k == 0), stop=(k == KD - 1), tile_position=tile)
                    last.then_inc(gu_mm, 1)
                    find(step + 2)
                    transposes(1 - u, i * 16 + 16 * (u + 1), step + 1, (0,))
                    pe.wait_ge(a_done, step + 1)
                    for j in range(2):
                        last = pe.transpose(ps_aT[:, j * P:(j + 1) * P], act_in[:, j:DE:2], m.ident[:, :])
                    last.then_inc(aT_mm, 1)
                    transposes(1 - u, i * 16 + 16 * (u + 1), step + 1, (1,))
                    pe.wait_ge(aT_done, step + 1)
                    for n in range(2):
                        pe.wait_ge((y_act, y_dve)[n], step + 1)
                        for j in range(2):
                            for at, place, tile in halves:
                                last = pe.matmul(ps_y[at, n, :], aT[:, j, at],
                                                 w_dn[:, place, j, n * 512:(n + 1) * 512].rearrange("p s n -> p (s n)"),
                                                 start=(j == 0), stop=(j == 1), tile_position=tile)
                        last.then_inc(dn_mm, 1)

                with pe.Fori(0, n_paired) as i:
                    for u in range(2):
                        step_of(i, u, True)
                with pe.Fori(n_paired, n_loops) as i:
                    for u in range(2):
                        step_of(i, u, False)


def build(nc, a, o):
    m = Memory()
    m.sems = []

    def sem(name):
        m.sems.append(nc.alloc_semaphore(name))
        return m.sems[-1]

    m.sem = sem
    constants(nc, m)
    for stage in (project, state_space_and_prompt_attention, sample_attention, mix_and_route, experts):
        stage(nc, a, o, m)
        end_stage(nc, m)


_OUTS = [("y_prompt", (1, SEQ, D)), ("y_sample", (DEC_B, DEC_S, D)),
         ("k_prompt", (1, 1, SEQ, NH, HD)), ("v_prompt", (1, 1, SEQ, NH, HD)), ("logf_prompt", (1, 1, SEQ, NH)),
         ("ssm_re_prompt", (1, 1, NG, NS)), ("ssm_im_prompt", (1, 1, NG, NS)),
         ("k_sample", (1, DEC_B, DEC_S, NH, HD)), ("v_sample", (1, DEC_B, DEC_S, NH, HD)), ("logf_sample", (1, DEC_B, DEC_S, NH)),
         ("ssm_re_sample", (1, DEC_B, NG, NS)), ("ssm_im_sample", (1, DEC_B, NG, NS))]


def kernel(**inputs):
    import numpy as _np
    import concourse.bacc as _bacc
    from concourse.bass_utils import run_bass_kernel_spmd as _run

    nc = _bacc.Bacc("TRN2", target_bir_lowering=False, num_devices=1)
    arrays, a, o = {}, {}, {}
    for name, value in inputs.items():
        x = _np.ascontiguousarray(value)
        arrays[f"in_{name}"] = x
        a[name] = nc.dram_tensor(f"in_{name}", x.shape, mybir.dt.from_np(x.dtype), kind="ExternalInput").ap()
    for name, shape in _OUTS:
        o[name] = nc.dram_tensor(f"out_{name}", shape, F32, kind="ExternalOutput").ap()
    build(nc, a, o)
    r = _run(nc, [arrays], core_ids=[0])
    return tuple(r.results[0][f"out_{name}"] for name, _ in _OUTS)
```
